# Optimizing a Trainium2 kernel written in Bass

```python
import math
import jax, jax.numpy as jnp
from jax import lax
import numpy as np

D_MODEL = 1024
BATCH = 1
SEQ = 512
DEPTH = 2

N_MIXERS = 2
DA_HEAD_DIM = 64
DA_HEADS = D_MODEL // (2 * DA_HEAD_DIM)
DA_QK_WIDTH = 2 * DA_HEADS * DA_HEAD_DIM
DA_V_WIDTH = DA_HEADS * 2 * DA_HEAD_DIM
Q_BLOCK = 128
ROPE_THETA = 10000.0
SG_CHUNK = 128
SG_GROUPS = 8
SG_HALF = 2 * D_MODEL
SG_GROUP_DIM = SG_HALF // SG_GROUPS
N_EXPERTS = 64
TOP_K = 6
N_EXPERT_GROUPS = 8
TOPK_GROUPS = 4
EXPERT_DIM = D_MODEL // 4
SHARED_DIM = EXPERT_DIM
ROUTED_SCALE = 2.5
MOE_BLOCK = 128
EPS = 1e-6

N_DA_LAYERS = (DEPTH + 1) // 2
N_SG_LAYERS = DEPTH // 2

kernel_name = "hybrid_diffattn_chunkgmlp_moe_adaln"

def rms_norm(x, g):
    xf = x.astype(jnp.float32)
    y = xf * lax.rsqrt(jnp.mean(xf * xf, axis=-1, keepdims=True) + EPS)
    return (y * g.astype(jnp.float32)).astype(x.dtype)

def layer_norm(x, g, b):
    xf = x.astype(jnp.float32)
    mu = jnp.mean(xf, axis=-1, keepdims=True)
    xc = xf - mu
    y = xc * lax.rsqrt(jnp.mean(xc * xc, axis=-1, keepdims=True) + EPS)
    return (y * g.astype(jnp.float32) + b.astype(jnp.float32)).astype(x.dtype)

def modulate(h, shift, scale):
    return h * (1 + scale[:, None, :]) + shift[:, None, :]

def apply_rope(x, cos, sin):
    x1, x2 = jnp.split(x, 2, axis=-1)
    c = cos[:, :, None, :]
    s = sin[:, :, None, :]
    return jnp.concatenate([x1 * c - x2 * s, x2 * c + x1 * s], axis=-1)

def diff_attention(h, positions, w_in, lam_q1, lam_k1, lam_q2, lam_k2, subln_g, w_out, lambda_init):
    B, S, _ = h.shape
    H, d = DA_HEADS, DA_HEAD_DIM
    qkv = h @ w_in
    q, k, v = jnp.split(qkv, [DA_QK_WIDTH, 2 * DA_QK_WIDTH], axis=-1)
    q = q.reshape(B, S, 2 * H, d)
    k = k.reshape(B, S, 2 * H, d)
    v = v.reshape(B, S, H, 2 * d)
    inv_freq = ROPE_THETA ** (-jnp.arange(0, d, 2, dtype=jnp.float32) / d)
    ang = positions.astype(jnp.float32)[..., None] * inv_freq
    cos = jnp.cos(ang).astype(h.dtype)
    sin = jnp.sin(ang).astype(h.dtype)
    q = apply_rope(q, cos, sin) * (d ** -0.5)
    k = apply_rope(k, cos, sin)
    f32 = jnp.float32
    lam = (jnp.exp(jnp.sum(lam_q1.astype(f32) * lam_k1.astype(f32)))
           - jnp.exp(jnp.sum(lam_q2.astype(f32) * lam_k2.astype(f32))) + lambda_init)
    nqb = S // Q_BLOCK
    qb = q.reshape(B, nqb, Q_BLOCK, 2 * H, d).transpose(1, 0, 2, 3, 4)

    def block(q_blk):
        s = jnp.einsum('bqhd,bkhd->bhqk', q_blk, k, preferred_element_type=jnp.float32)
        p = jax.nn.softmax(s, axis=-1).reshape(B, H, 2, Q_BLOCK, S)
        a = (p[:, :, 0] - lam * p[:, :, 1]).astype(v.dtype)
        return jnp.einsum('bhqk,bkhe->bqhe', a, v)

    o = lax.map(block, qb)
    o = o.transpose(1, 0, 2, 3, 4).reshape(B, S, H, 2 * d)
    o = rms_norm(o, subln_g) * (1.0 - lambda_init)
    return o.reshape(B, S, H * 2 * d) @ w_out

def chunked_spatial_gating(h, w_in, ln_g, ln_b, w_s, b_s, w_out):
    B, S, _ = h.shape
    z = jax.nn.gelu(h @ w_in, approximate=False)
    u, v = jnp.split(z, 2, axis=-1)
    v = layer_norm(v, ln_g, ln_b)
    n = S // SG_CHUNK
    v = v.reshape(B, n, SG_CHUNK, SG_GROUPS, SG_GROUP_DIM)
    s = jnp.einsum('gpq,bnqgc->bnpgc', w_s, v) + b_s.T[None, None, :, :, None]
    return (u * s.reshape(B, S, SG_HALF)) @ w_out

def moe(h, w_router, router_bias, w_gate, w_up, w_down, ws_gate, ws_up, ws_down):
    B, S, D = h.shape
    T = B * S
    xf = h.reshape(T, D)
    logits = jnp.dot(xf, w_router, preferred_element_type=jnp.float32)
    scores = jax.nn.sigmoid(logits)
    sel = scores + router_bias.astype(jnp.float32)
    grp = sel.reshape(T, N_EXPERT_GROUPS, N_EXPERTS // N_EXPERT_GROUPS)
    grp_score = jnp.sum(lax.top_k(grp, 2)[0], axis=-1)
    _, gidx = lax.top_k(grp_score, TOPK_GROUPS)
    gmask = jnp.sum(jax.nn.one_hot(gidx, N_EXPERT_GROUPS, dtype=jnp.float32), axis=1) > 0
    emask = jnp.repeat(gmask, N_EXPERTS // N_EXPERT_GROUPS, axis=1)
    _, eidx = lax.top_k(jnp.where(emask, sel, -jnp.inf), TOP_K)
    wts = jnp.take_along_axis(scores, eidx, axis=1)
    wts = wts / jnp.sum(wts, axis=-1, keepdims=True) * ROUTED_SCALE
    TK = T * TOP_K
    flat_e = eidx.reshape(TK)
    flat_tok = jnp.arange(TK, dtype=jnp.int32) // TOP_K
    flat_w = wts.reshape(TK).astype(h.dtype)
    order = jnp.argsort(flat_e)
    se = flat_e[order]
    counts = jnp.bincount(flat_e, length=N_EXPERTS)
    padded = (counts + MOE_BLOCK - 1) // MOE_BLOCK * MOE_BLOCK
    pad_end = jnp.cumsum(padded)
    pad_start = pad_end - padded
    start = jnp.cumsum(counts) - counts
    dest = pad_start[se] + jnp.arange(TK, dtype=jnp.int32) - start[se]
    nb = TK // MOE_BLOCK + N_EXPERTS
    P = nb * MOE_BLOCK
    buf_tok = jnp.zeros((P,), jnp.int32).at[dest].set(flat_tok[order])
    buf_w = jnp.zeros((P,), h.dtype).at[dest].set(flat_w[order])
    block_e = jnp.minimum(
        jnp.searchsorted(pad_end, jnp.arange(nb, dtype=pad_end.dtype) * MOE_BLOCK, side='right'),
        N_EXPERTS - 1)
    y0 = (jax.nn.silu(xf @ ws_gate) * (xf @ ws_up)) @ ws_down

    def step(y, blk):
        tok, e, w = blk
        xb = xf[tok]
        hb = jax.nn.silu(xb @ w_gate[e]) * (xb @ w_up[e])
        return y.at[tok].add((hb @ w_down[e]) * w[:, None]), None

    y, _ = lax.scan(step, y0, (buf_tok.reshape(nb, MOE_BLOCK), block_e,
                               buf_w.reshape(nb, MOE_BLOCK)))
    return y.reshape(B, S, D)

def setup_inputs(seed: int = 0) -> dict:
    key = jax.random.key(seed)
    ks = iter(jax.random.split(key, 32))
    nrm = lambda shape, s: jax.random.normal(next(ks), shape, jnp.float32) * s
    D, E, F = D_MODEL, N_EXPERTS, EXPERT_DIM
    NA, NS = N_DA_LAYERS, N_SG_LAYERS
    return {
        "x": nrm((BATCH, SEQ, D), 1.0),
        "c": nrm((BATCH, D), 1.0),
        "positions": jnp.broadcast_to(jnp.arange(SEQ, dtype=jnp.int32), (BATCH, SEQ)),
        "norm1_g": 1.0 + nrm((DEPTH, D), 0.02),
        "norm2_g": 1.0 + nrm((DEPTH, D), 0.02),
        "ada_w": nrm((DEPTH, D, 6 * D), 0.5 * D ** -0.5),
        "ada_b": nrm((DEPTH, 6 * D), 0.02),
        "da_w_in": nrm((NA, D, 2 * DA_QK_WIDTH + DA_V_WIDTH), D ** -0.5),
        "da_lam_q1": nrm((NA, DA_HEAD_DIM), 0.1),
        "da_lam_k1": nrm((NA, DA_HEAD_DIM), 0.1),
        "da_lam_q2": nrm((NA, DA_HEAD_DIM), 0.1),
        "da_lam_k2": nrm((NA, DA_HEAD_DIM), 0.1),
        "da_subln_g": 1.0 + nrm((NA, 2 * DA_HEAD_DIM), 0.02),
        "da_w_out": nrm((NA, DA_V_WIDTH, D), DA_V_WIDTH ** -0.5),
        "sg_w_in": nrm((NS, D, 2 * SG_HALF), D ** -0.5),
        "sg_ln_g": 1.0 + nrm((NS, SG_HALF), 0.02),
        "sg_ln_b": nrm((NS, SG_HALF), 0.02),
        "sg_w_s": nrm((NS, SG_GROUPS, SG_CHUNK, SG_CHUNK), SG_CHUNK ** -0.5),
        "sg_b_s": nrm((NS, SG_GROUPS, SG_CHUNK), 0.02),
        "sg_w_out": nrm((NS, SG_HALF, D), SG_HALF ** -0.5),
        "moe_w_router": nrm((DEPTH, D, E), D ** -0.5),
        "moe_router_bias": nrm((DEPTH, E), 0.01),
        "moe_w_gate": nrm((DEPTH, E, D, F), D ** -0.5),
        "moe_w_up": nrm((DEPTH, E, D, F), D ** -0.5),
        "moe_w_down": nrm((DEPTH, E, F, D), F ** -0.5),
        "moe_ws_gate": nrm((DEPTH, D, SHARED_DIM), D ** -0.5),
        "moe_ws_up": nrm((DEPTH, D, SHARED_DIM), D ** -0.5),
        "moe_ws_down": nrm((DEPTH, SHARED_DIM, D), SHARED_DIM ** -0.5),
        "final_g": 1.0 + nrm((D,), 0.02),
    }

def reference(x, c, positions, norm1_g, norm2_g, ada_w, ada_b,
              da_w_in, da_lam_q1, da_lam_k1, da_lam_q2, da_lam_k2, da_subln_g, da_w_out,
              sg_w_in, sg_ln_g, sg_ln_b, sg_w_s, sg_b_s, sg_w_out,
              moe_w_router, moe_router_bias, moe_w_gate, moe_w_up, moe_w_down,
              moe_ws_gate, moe_ws_up, moe_ws_down, final_g):
    cond = jax.nn.silu(c)
    for i in range(DEPTH):
        mod = cond @ ada_w[i] + ada_b[i]
        sh1, sc1, g1, sh2, sc2, g2 = jnp.split(mod, 6, axis=-1)
        h = modulate(rms_norm(x, norm1_g[i]), sh1, sc1)
        j = i // N_MIXERS
        if i % N_MIXERS == 0:
            lambda_init = 0.8 - 0.6 * math.exp(-0.3 * i)
            mix = diff_attention(h, positions, da_w_in[j], da_lam_q1[j], da_lam_k1[j],
                                 da_lam_q2[j], da_lam_k2[j], da_subln_g[j], da_w_out[j],
                                 lambda_init)
        else:
            mix = chunked_spatial_gating(h, sg_w_in[j], sg_ln_g[j], sg_ln_b[j],
                                         sg_w_s[j], sg_b_s[j], sg_w_out[j])
        x = x + g1[:, None, :] * mix
        h = modulate(rms_norm(x, norm2_g[i]), sh2, sc2)
        x = x + g2[:, None, :] * moe(h, moe_w_router[i], moe_router_bias[i], moe_w_gate[i],
                                     moe_w_up[i], moe_w_down[i], moe_ws_gate[i],
                                     moe_ws_up[i], moe_ws_down[i])
    return rms_norm(x, final_g)


_drawn_inputs = setup_inputs


def setup_inputs(seed=0):
    import zlib

    import numpy as np

    out = dict(_drawn_inputs(seed))
    spreads = {}
    factors = {'da_lam_q2': 3.147,
     'da_lam_k2': 8.0,
     'sg_ln_g': 3.447,
     'sg_ln_b': 4.106,
     'sg_b_s': 4.104,
     'final_g': 3.148}
    for name, (base, spread) in spreads.items():
        noise = np.random.default_rng([zlib.crc32(name.encode()), seed]).standard_normal(out[name].shape)
        drawn = base * np.exp(spread * noise) if base else spread * noise
        out[name] = __import__('jax').numpy.asarray(drawn.astype(out[name].dtype))
    for name, factor in factors.items():
        out[name] = (out[name] * factor).astype(out[name].dtype)
    return out
```

```python
import math
from contextlib import ExitStack

import concourse.bass as bass
from concourse import mybir

FP32 = mybir.dt.float32
I32 = mybir.dt.int32
ALU = mybir.AluOpType
ACT = mybir.ActivationFunctionType
AX = mybir.AxisListType

P = 128
D = 1024
S = 512
NT = S // P
KC = D // P
EPS = 1e-6
BANK = 512

HEADS = 8
HD = 64
LAMBDA_INIT = 0.8 - 0.6 * math.exp(-0.3 * 0)
THETA = 10000.0

SG_HALF = 2 * D
GROUPS = 8
GROUP_DIM = SG_HALF // GROUPS

E = 64
F = D // 4
TOP_K = 6
EXPERT_GROUPS = 8
TOPK_GROUPS = 4
ROUTED_SCALE = 2.5
RING = 4
SLOT = 3 * KC * F
SLOTS_PER_BLOCK = P
NARROW = 64
MAX_OVERFLOW = S * TOP_K // SLOTS_PER_BLOCK
PAD = 32
SKIP = 4096.0


class Shared:
    pass


def ds(start, size):
    return bass.ds(start, size)


def after(engine, semaphore, count):
    if not (isinstance(count, int) and count <= 0):
        engine.wait_ge(semaphore, count)


class Chain:

    def __init__(self, engine, semaphore, base=0):
        self.engine, self.semaphore, self.base, self.n = engine, semaphore, base, 0

    def __call__(self, instruction):
        instruction.then_inc(self.semaphore, 1)
        self.n += 1
        self.engine.wait_ge(self.semaphore, self.base + self.n)


ADA_HALF = KC // 2


def ada_buffer(g, half):
    return g.ring[:, half, 0:ADA_HALF * D].rearrange("p (k n) -> p k n", n=D)


def load_ada(g, eng, n, half, loaded):
    rows = g.inputs["ada_w"][ds(n, 1), :, :].rearrange("a (p k) n -> p (a k) n", k=KC)
    eng.dma_start(ada_buffer(g, half), rows[:, half * ADA_HALF:(half + 1) * ADA_HALF, :]).then_inc(loaded, 16)


def add_ada(nc, g, dve, chunks, chain_s, count, last_of_half, last_of_row):
    for k in chunks:
        w, cond = ada_buffer(g, k // ADA_HALF)[:, k % ADA_HALF, :], g.cond[:, k:k + 1]
        if k:
            dve.wait_ge(chain_s, KC * count + k)
            op = nc.vector.scalar_tensor_tensor(g.partial[:], w, cond, g.partial[:], ALU.mult, ALU.add)
        else:
            op = nc.vector.tensor_scalar(g.partial[:], w, cond, None, ALU.mult)
        op.then_inc(chain_s, 1)
        if k % ADA_HALF == ADA_HALF - 1:
            dve.wait_ge(chain_s, KC * count + k + 1)
            dve.sem_inc(last_of_half, 1)
        if k == KC - 1:
            dve.sem_inc(last_of_row, 1)


def conditioning(nc, g):
    A = g.inputs
    with ExitStack() as scope:
        sb = lambda n, s, d=FP32: scope.enter_context(nc.sbuf_tensor(n, s, d))
        c_cols = sb("c_cols", [P, KC])
        pos_i = sb("pos_i", [P, S], I32)
        pos_f = sb("pos_f", [P, S])
        angle = sb("angle", [P, S])
        turns = sb("turns", [P, S])
        inv_freq = sb("inv_freq", [P, 1])
        half_pi = sb("half_pi", [P, 1])
        lam_in = sb("lam_in", [P, 4, HD])
        lam_prod = sb("lam_prod", [P, 2, HD])
        lam_sum = sb("lam_sum", [P, 2])
        lam_exp = sb("lam_exp", [P, 2])
        iota_i = sb("iota_i", [P, S], I32)
        sem = g.stage_semaphores(scope, "")
        c_loaded, cond_done = sem("c_loaded"), sem("cond_done")
        ada_loaded = [sem(f"ada_loaded{i}") for i in range(2)]
        ada_used, ada_chain, partial_done, partial_stored = sem("ada_used"), sem("ada_chain"), sem("partial_done"), sem("partial_stored")
        small_loaded, consts_built, iota_built = g.sem("small_loaded"), sem("consts_built"), sem("iota_built")
        chain_s, angle_done, abs_done, trig_done = sem("dve_chain0"), sem("angle_done"), sem("abs_done"), sem("trig_done")
        lam_summed, lam_exped = sem("lam_summed"), sem("lam_exped")
        x_loaded = sem("x_loaded")
        block = scope.enter_context(nc.Block())

        @block.sync
        def _(sp):
            sp.dma_start(c_cols[:], A["c"].rearrange("a (p k) -> p (a k)", k=KC)).then_inc(c_loaded, 16)
            for half in range(2):
                load_ada(g, sp, 0, half, ada_loaded[half])
            sp.dma_start(g.x[:, :, :], A["x"][0, :, :].rearrange("(t p) d -> p t d", p=P)).then_inc(x_loaded, 16)
            for half in range(2):
                sp.wait_ge(ada_used, half + 1)
                load_ada(g, sp, 1, half, ada_loaded[half])
            for n in range(2):
                sp.wait_ge(partial_done, n + 1)
                sp.dma_start(g.mod_dram[n, :, :], g.partial[:]).then_inc(partial_stored, 16)
            sp.wait_ge(partial_stored, 32)
            sp.wait_ge(x_loaded, 16)

        @block.gpsimd
        def _(pool):
            pool.sem_clear(g.other_semaphores)
            pool.dma_start(pos_i[:], A["positions"][0, :].partition_broadcast(P)).then_inc(small_loaded, 16)
            pool.dma_start(inv_freq[:], A["rope_inv_freq"]).then_inc(small_loaded, 16)
            for i, name in enumerate(("da_lam_q1", "da_lam_k1", "da_lam_q2", "da_lam_k2")):
                pool.dma_start(lam_in[:, i, :], A[name][0, :].partition_broadcast(P)).then_inc(small_loaded, 16)
            pool.dma_start(g.subln[:], A["da_subln_g"].rearrange("a p -> p a")).then_inc(small_loaded, 16)
            pool.memset(g.ident[:], 0.0).then_inc(consts_built, 1)
            pool.memset(g.tri[:], 1.0).then_inc(consts_built, 1)
            pool.memset(g.group_lower[:], 1.0).then_inc(consts_built, 1)
            pool.wait_ge(consts_built, 3)
            pool.affine_select(out=g.ident[:], in_=g.ident[:], compare_op=ALU.not_equal, fill=1.0, base=0,
                               pattern=[[-1, P]], channel_multiplier=1).then_inc(consts_built, 1)
            pool.affine_select(out=g.tri[:], in_=g.tri[:], compare_op=ALU.is_gt, fill=0.0, base=0,
                               pattern=[[1, P]], channel_multiplier=-1).then_inc(consts_built, 1)
            pool.affine_select(out=g.group_lower[:], in_=g.group_lower[:], compare_op=ALU.is_gt, fill=0.0, base=0,
                               pattern=[[1, EXPERT_GROUPS], [-1, EXPERT_GROUPS]], channel_multiplier=0)\
                .then_inc(consts_built, 1)
            pool.memset(g.ones[:], 1.0).then_inc(consts_built, 1)
            pool.iota(iota_i[:], pattern=[[1, S]], base=0, channel_multiplier=0).then_inc(iota_built, 1)
            pool.iota(g.tok_i[:], pattern=[[P, NT]], base=0, channel_multiplier=1).then_inc(iota_built, 1)

        @block.scalar
        def _(act):
            act.wait_ge(c_loaded, 16)
            nc.scalar.activation(g.cond[:], c_cols[:], ACT.Silu).then_inc(cond_done, 1)
            act.wait_ge(lam_summed, 1)
            nc.scalar.activation(lam_exp[:], lam_sum[:], ACT.Exp).then_inc(lam_exped, 1)
            act.wait_ge(angle_done, 1)
            nc.scalar.activation(turns[:], angle[:], ACT.Abs).then_inc(abs_done, 1)
            act.wait_ge(abs_done, 1)
            nc.scalar.activation(g.cos[:], turns[:], ACT.Sin, bias=half_pi[:], scale=-1.0).then_inc(trig_done, 1)
            for q in range(4):
                rows = slice(32 * q, 32 * q + 32)
                nc.scalar.activation(g.sin[rows, :], angle[rows, :], ACT.Sin, scale=-1.0 if q % 2 else 1.0)\
                    .then_inc(trig_done, 1)

        @block.vector
        def _(dve):
            chain = Chain(dve, chain_s)
            dve.wait_ge(small_loaded, 7 * 16)
            chain(nc.vector.tensor_tensor(lam_prod[:], lam_in[:, 0:4:2, :], lam_in[:, 1:4:2, :], ALU.mult))
            nc.vector.reduce_sum(lam_sum[:], lam_prod[:], AX.X).then_inc(lam_summed, 1)
            nc.vector.memset(half_pi[:], math.pi / 2)
            chain(nc.vector.tensor_copy(pos_f[:], pos_i[:]))
            chain(nc.vector.tensor_scalar(angle[:], pos_f[:], inv_freq[:], None, ALU.mult))
            magic = 1.5 * 2.0 ** 23
            chain(nc.vector.tensor_scalar(turns[:], angle[:], 1.0 / (2 * math.pi), magic, ALU.mult, ALU.add))
            chain(nc.vector.tensor_scalar(turns[:], turns[:], -magic, None, ALU.add))
            first = 6.28125
            second = math.floor((2 * math.pi - first) * 2 ** 22) / 2 ** 22
            third = 2 * math.pi - first - second
            for part in (first, second, third):
                chain(nc.vector.scalar_tensor_tensor(angle[:], turns[:], -part, angle[:], ALU.mult, ALU.add))
            nc.vector.tensor_scalar(angle[:], angle[:], 3.1415925, -3.1415925, ALU.min, ALU.max).then_inc(angle_done, 1)
            dve.wait_ge(iota_built, 2)
            nc.vector.tensor_copy(g.iota[:], iota_i[:])
            chain(nc.vector.tensor_copy(g.tok[:], g.tok_i[:]))
            nc.vector.tensor_scalar(g.tok_shift[:], g.tok[:], -SKIP, None, ALU.add)
            nc.vector.tensor_scalar(g.row_shift[:], g.tok[:], float(TOP_K), -SKIP, ALU.mult, ALU.add)
            nc.vector.tensor_scalar(g.subln[:], g.subln[:], 1.0 - LAMBDA_INIT, None, ALU.mult)
            nc.vector.memset(g.prefix[:], 0.0)
            dve.wait_ge(lam_exped, 1)
            chain(nc.vector.tensor_tensor(g.neg_lam[:], lam_exp[:, 1:2], lam_exp[:, 0:1], ALU.subtract))
            chain(nc.vector.tensor_scalar(g.neg_lam[:], g.neg_lam[:], -LAMBDA_INIT, None, ALU.add))
            dve.wait_ge(cond_done, 1)
            for n in range(2):
                if n:
                    dve.wait_ge(partial_stored, 16)
                for half in range(2):
                    dve.wait_ge(ada_loaded[half], 16 * n + 16)
                    add_ada(nc, g, dve, range(half * ADA_HALF, (half + 1) * ADA_HALF), ada_chain, n, ada_used, partial_done)


def store_partials(g, pool, first, rows, done, stored, free):
    pool.sem_inc(free, 1)
    with pool.Fori(0, rows) as n:
        pool.wait_ge(done, n + 1)
        pool.dma_start(g.mod_dram[ds(first + n, 1), :, :].rearrange("a p n -> p (a n)"), g.partial[:]).then_inc(stored, 16)
        pool.wait_ge(stored, 16 * n + 16)
        pool.sem_inc(free, 1)


def sum_conditioning(nc, g, partial, ada_b, ps):
    for n in range(D // BANK):
        cols = slice(n * BANK, (n + 1) * BANK)
        nc.tensor.matmul(ps[:, cols], g.ones[:], partial[:, cols], start=True, stop=False)
        last = nc.tensor.matmul(ps[:, cols], g.ones[0:1, :], ada_b[:, cols], start=False, stop=True)
    return last


def normalise(nc, g, tag, layer, which, n_rows, to_dram, load_ahead):
    A = g.inputs
    norm_g = A["norm1_g" if which == 0 else "norm2_g"][layer, :]
    with ExitStack() as scope:
        sb = lambda n, s, d=FP32: scope.enter_context(nc.sbuf_tensor(f"{tag}_{n}", s, d))
        partial = sb("partial", [P, n_rows, D])
        ada_b = sb("ada_b", [1, n_rows * D])
        scale = sb("scale", [P, D])
        gain = sb("gain", [P, D])
        squares = sb("squares", [P, D])
        h = sb("h", [P, 2, D])
        sums, mean_sq, std, rstd = sb("sums", [P, NT]), sb("mean_sq", [P, NT]), sb("std", [P, NT]), sb("rstd", [P, NT])
        ps_t = [scope.enter_context(nc.psum_tensor(f"{tag}_ps{i}", [P, 4, P], FP32)) for i in range(2)]
        ps_mod = [scope.enter_context(nc.psum_tensor(f"{tag}_mod{i}", [P, D], FP32)) for i in range(n_rows)]
        sem = g.stage_semaphores(scope, f"{tag}_")
        gain_loaded, bias_loaded, partial_loaded = sem("gain_loaded"), sem("bias_loaded"), [sem(f"partial_loaded{i}") for i in range(n_rows)]
        rows_summed, squared, mean_done, std_done = sem("rows_summed"), sem("squared"), sem("mean_done"), sem("std_done")
        chain_s, h_done, transposed = sem("chain"), sem("h_done"), sem("transposed")
        act_copied, dve_copied, h_stored = sem("act_copied"), sem("dve_copied"), [g.sem(f"h_stored{layer}_{i}") for i in range(2)]
        block = scope.enter_context(nc.Block())

        @block.sync
        def _(sp):
            first = 6 * layer + 3 * which
            sp.dma_start(ada_b[:], A["ada_b"][layer:layer + 1, 3 * which * D:(3 * which + n_rows) * D]).then_inc(bias_loaded, 16)
            for i in (1, 0, 2)[:n_rows]:
                sp.dma_start(partial[:, i, :], g.mod_dram[first + i, :, :]).then_inc(partial_loaded[i], 16)
                if i == 1:
                    sp.dma_start(gain[:], norm_g.partition_broadcast(P)).then_inc(gain_loaded, 16)
            load_ahead(sp)
            sp.wait_ge(gain_loaded, 16)

        @block.gpsimd
        def _(pool):
            pool.sem_clear(g.other_semaphores)
            if to_dram:
                for t in range(NT):
                    pool.wait_ge(h_done, t + 1)
                    pool.dma_start(g.h_dram[t * P:(t + 1) * P, :], h[:, t % 2, :]).then_inc(h_stored[t % 2], 16)
                for i in range(2):
                    pool.wait_ge(h_stored[i], 16 * NT // 2)

        @block.scalar
        def _(act):
            for t in range(NT):
                nc.scalar.activation(squares[:], g.x[:, t, :], ACT.Square, accum_out=sums[:, t:t + 1])\
                    .then_inc(squared, 1)
                act.wait_ge(squared, t + 1)
            act.wait_ge(mean_done, 1)
            nc.scalar.activation(std[:], mean_sq[:], ACT.Sqrt).then_inc(std_done, 1)
            for t in range(NT):
                act.wait_ge(transposed, 2 * t + 1)
                nc.scalar.activation(g.hT[:, 0:4, t * P:(t + 1) * P], ps_t[0][:], ACT.Copy).then_inc(act_copied, 1)
            if n_rows == 3:
                act.wait_ge(rows_summed, 3)
                nc.scalar.activation(g.gate[:], ps_mod[2][:], ACT.Copy)

        @block.tensor
        def _(pe):
            pe.wait_ge(bias_loaded, 16)

            def sum_row(i):
                pe.wait_ge(partial_loaded[i], 16)
                sum_conditioning(nc, g, partial[:, i, :], ada_b[:, i * D:(i + 1) * D], ps_mod[i]).then_inc(rows_summed, 1)

            sum_row(1)
            sum_row(0)
            for t in range(NT):
                if t == 1 and n_rows == 3:
                    sum_row(2)
                pe.wait_ge(h_done, t + 1)
                for half in range(2):
                    if t:
                        pe.wait_ge((act_copied, dve_copied)[half], t)
                    for i in range(4):
                        last = nc.tensor.transpose(ps_t[half][:, i, :], h[:, t % 2, 4 * half + i::KC], g.ident[:])
                    last.then_inc(transposed, 1)

        @block.vector
        def _(dve):
            chain = Chain(dve, chain_s)
            dve.wait_ge(squared, NT)
            nc.vector.tensor_scalar(mean_sq[:], sums[:], 1.0 / D, EPS, ALU.mult, ALU.add).then_inc(mean_done, 1)
            dve.wait_ge(gain_loaded, 16)
            dve.wait_ge(rows_summed, 1)
            chain(nc.vector.scalar_tensor_tensor(scale[:], ps_mod[1][:], 1.0, gain[:], ALU.add, ALU.mult))
            dve.wait_ge(std_done, 1)
            chain(nc.vector.reciprocal(rstd[:], std[:]))

            def copy_out(t):
                dve.wait_ge(transposed, 2 * t + 2)
                nc.vector.tensor_copy(g.hT[:, 4:8, t * P:(t + 1) * P], ps_t[1][:]).then_inc(dve_copied, 1)

            for t in range(NT):
                if t >= 2:
                    dve.wait_ge(transposed, 2 * (t - 1))
                    if to_dram:
                        dve.wait_ge(h_stored[t % 2], 16 * (t // 2))
                chain(nc.vector.scalar_tensor_tensor(h[:, t % 2, :], g.x[:, t, :], rstd[:, t:t + 1], scale[:],
                                                     ALU.mult, ALU.mult))
                if t == 0:
                    dve.wait_ge(rows_summed, 2)
                nc.vector.tensor_tensor(h[:, t % 2, :], h[:, t % 2, :], ps_mod[0][:], ALU.add).then_inc(h_done, 1)
                if t:
                    copy_out(t - 1)
            copy_out(NT - 1)


def attention_buffers(nc, g, scope):
    sb = lambda n, s, d=FP32: scope.enter_context(nc.sbuf_tensor(n, s, d))
    b = Shared()
    b.wq, b.wk, b.wv, b.wo = sb("wq", [P, KC, P]), sb("wk", [P, KC, P]), sb("wv", [P, KC, P]), sb("wo", [P, HEADS, D])
    b.q_loaded, b.k_loaded, b.v_loaded, b.wo_loaded = (g.sem(n) for n in ("q_loaded", "k_loaded", "v_loaded", "wo_loaded"))
    return b


def load_head(g, b, eng, h, part):
    w = g.inputs["da_w_in"][0, :, :].rearrange("(p k) (s h n) -> p k s h n", k=KC, s=3, n=P)
    dst, loaded = ((b.wq, b.q_loaded), (b.wk, b.k_loaded), (b.wv, b.v_loaded))[part]
    eng.dma_start(dst[:], w[:, :, part, ds(h, 1), :].rearrange("p k a n -> p k (a n)")).then_inc(loaded, 16)


def attention(nc, g, b):
    with ExitStack() as scope:
        sb = lambda n, s, d=FP32: scope.enter_context(nc.sbuf_tensor(n, s, d))
        qT, kT, v = sb("qT", [P, S]), sb("kT", [P, S]), sb("v", [P, NT, P])
        rot, rot2 = sb("rot", [P, S]), sb("rot2", [P, S])
        prob = sb("prob", [P, 8, S])
        neg_max, row_sum, inv_sum, lam_inv = (sb(n, [P, 8]) for n in ("neg_max", "row_sum", "inv_sum", "lam_inv"))
        aT = [sb(f"aT{i}", [P, NT, P]) for i in range(NT)]
        osq, on = sb("osq", [P, NT, P]), sb("on", [P, NT, P])
        o_sum, o_ms, o_std, o_inv = (sb(n, [P, NT]) for n in ("o_sum", "o_ms", "o_std", "o_inv"))
        oT = sb("oT", [P, HEADS, S])
        mix = sb("mix", [P, 2, BANK])
        gate_b = sb("gate_b", [1, D])
        ps_s = [scope.enter_context(nc.psum_tensor(f"ps_s{i}", [P, BANK], FP32)) for i in range(4)]
        ps_kv = scope.enter_context(nc.psum_tensor("ps_kv", [P, 2 * BANK], FP32))
        ps_k, ps_v = ps_kv[:, 0:BANK], ps_kv[:, BANK:]
        ps_q, ps_o = (scope.enter_context(nc.psum_tensor(n, [P, BANK], FP32)) for n in ("ps_q", "ps_o"))
        sem = g.stage_semaphores(scope, "")
        qk_projected, v_projected, v_copied, rotated = sem("qk_projected"), sem("v_projected"), sem("v_copied"), sem("rotated")
        scored, maxed, exped, mixed = sem("scored"), sem("maxed"), sem("exped"), sem("mixed")
        a_transposed, a_copied, weighted, o_squared = sem("a_transposed"), sem("a_copied"), sem("weighted"), sem("o_squared")
        o_mean, o_rooted, o_normed, o_transposed = sem("o_mean"), sem("o_rooted"), sem("o_normed"), sem("o_transposed")
        o_copied, chain_s, projected_out, added = sem("o_copied"), sem("att_chain"), sem("projected_out"), sem("att_added")
        ada_loaded, ada_used, ada_chain = [sem(f"ada_loaded{i}") for i in range(2)], sem("ada_used"), sem("ada_chain")
        partial_done, partial_free, partial_stored = sem("partial_done"), sem("partial_free"), g.sem("partial_stored0")
        gate_loaded, gate_summed, gate_done = sem("gate_loaded"), sem("gate_summed"), sem("gate_done")
        block = scope.enter_context(nc.Block())
        FIRST_ADA, ADA_ROWS = 2, HEADS - 1
        HOPS = 10

        @block.gpsimd
        def _(pool):
            pool.sem_clear(g.other_semaphores)
            store_partials(g, pool, FIRST_ADA, ADA_ROWS, partial_done, partial_stored, partial_free)

        @block.sync
        def _(sp):
            sp.dma_start(gate_b[:], g.inputs["ada_b"][0:1, 2 * D:3 * D]).then_inc(gate_loaded, 16)
            sp.dma_start(b.wo[:], g.inputs["da_w_out"][0, :, :].rearrange("(h p) n -> p h n", p=P)).then_inc(b.wo_loaded, 16)
            with sp.Fori(1, HEADS) as h:
                sp.wait_ge(qk_projected, 2 * h - 1)
                load_head(g, b, sp, h, 0)
                sp.wait_ge(qk_projected, 2 * h)
                load_head(g, b, sp, h, 1)
                sp.wait_ge(v_projected, h)
                load_head(g, b, sp, h, 2)
                for half in range(2):
                    sp.wait_ge(ada_used, 2 * (h - 1) + half + 1)
                    load_ada(g, sp, FIRST_ADA + h - 1, half, ada_loaded[half])
            sp.wait_ge(ada_used, 2 * ADA_ROWS + 2)
            sp.wait_ge(partial_free, ADA_ROWS + 1)
            sp.dma_start(g.partial[:], g.mod_dram[2, :, :]).then_inc(gate_loaded, 16)
            g.load_expert(sp, 0, 0, 0)
            g.load_expert(sp, 0, 1, 1)

        @block.tensor
        def _(pe):
            def project_qk(h):
                pe.wait_ge(o_copied, h + 1)
                for w, loaded, ps in ((b.wq, b.q_loaded, ps_q), (b.wk, b.k_loaded, ps_k)):
                    pe.wait_ge(loaded, 16 * h + 16)
                    for k in range(KC):
                        last = nc.tensor.matmul(ps[:], w[:, k, :], g.hT[:, k, :], start=(k == 0), stop=(k == KC - 1))
                    last.then_inc(qk_projected, 1)

            def project_v(h):
                pe.wait_ge(b.v_loaded, 16 * h + 16)
                for t in range(NT):
                    for k in range(KC):
                        last = nc.tensor.matmul(ps_v[:, t * P:(t + 1) * P], g.hT[:, k, t * P:(t + 1) * P], b.wv[:, k, :],
                                                start=(k == 0), stop=(k == KC - 1))
                last.then_inc(v_projected, 1)

            def scores(h):
                pe.wait_ge(rotated, 2 * h + 2)
                for u in range(8):
                    t, c = divmod(u, 2)
                    if u < 4:
                        pe.wait_ge(a_copied, 4 * h + u + 1)
                    else:
                        pe.wait_ge(exped, 8 * h + u - 3)
                    rows = slice(HD * c, HD * c + HD)
                    nc.tensor.matmul(ps_s[u % 4][:], qT[rows, t * P:(t + 1) * P], kT[rows, :], start=True, stop=True)\
                        .then_inc(scored, 1)

            def transpose_probs(h, t):
                pe.wait_ge(mixed, 4 * h + t + 1)
                for c in range(NT):
                    last = nc.tensor.transpose(ps_s[t][:, c * P:(c + 1) * P], prob[:, 2 * t, c * P:(c + 1) * P], g.ident[:])
                last.then_inc(a_transposed, 1)

            def weigh_values(h, t):
                pe.wait_ge(a_copied, 4 + 4 * h + t + 1)
                if t == 0:
                    pe.wait_ge(v_copied, h + 1)
                    pe.wait_ge(o_normed, h + 1)
                for c in range(NT):
                    last = nc.tensor.matmul(ps_o[:, t * P:(t + 1) * P], aT[t][:, c, :], v[:, c, :],
                                            start=(c == 0), stop=(c == NT - 1))
                if t == NT - 1:
                    last.then_inc(weighted, 1)

            def values(h):
                transpose_probs(h, 0)
                for t in range(1, NT):
                    transpose_probs(h, t)
                    weigh_values(h, t - 1)
                weigh_values(h, NT - 1)

            def transpose_outputs(h):
                pe.wait_ge(o_normed, h + 2)
                for t in range(NT):
                    last = nc.tensor.transpose(ps_q[:, t * P:(t + 1) * P], on[:, t, :], g.ident[:])
                last.then_inc(o_transposed, 1)

            project_qk(0)
            project_v(0)
            with pe.Fori(0, HEADS - 1) as h:
                scores(h)
                project_qk(h + 1)
                values(h)
                project_v(h + 1)
                pe.wait_ge(rotated, 2 * h + 3)
                transpose_outputs(h)
            scores(HEADS - 1)
            pe.wait_ge(gate_loaded, 32)
            pe.wait_ge(v_copied, HEADS)
            sum_conditioning(nc, g, g.partial, gate_b, ps_kv).then_inc(gate_summed, 1)
            values(HEADS - 1)
            transpose_outputs(HEADS - 1)
            pe.wait_ge(b.wo_loaded, 16)
            pe.wait_ge(o_copied, 2 + HEADS)
            pe.wait_ge(gate_done, 1)
            for i, ps in enumerate([*ps_s, ps_k, ps_v, ps_o, ps_q]):
                t, n = divmod(i, 2)
                for h in range(HEADS):
                    last = nc.tensor.matmul(ps[:], oT[:, h, t * P:(t + 1) * P], b.wo[:, h, n * BANK:(n + 1) * BANK],
                                            start=(h == 0), stop=(h == HEADS - 1))
                last.then_inc(projected_out, 1)

        @block.scalar
        def _(act):
            def copy_v(h):
                act.wait_ge(v_projected, h + 1)
                nc.scalar.activation(v[:].rearrange("p t n -> p (t n)"), ps_v, ACT.Copy).then_inc(v_copied, 1)

            def head(h, last):
                for u in range(8):
                    act.wait_ge(maxed, 8 * h + u + 1)
                    nc.scalar.activation(prob[:, u, :], ps_s[u % 4][:], ACT.Exp, bias=neg_max[:, u:u + 1],
                                         accum_out=row_sum[:, u:u + 1]).then_inc(exped, 1)
                for t in range(NT):
                    act.wait_ge(a_transposed, 4 * h + t + 1)
                    nc.scalar.activation(aT[t][:].rearrange("p c n -> p (c n)"), ps_s[t][:], ACT.Copy).then_inc(a_copied, 1)
                act.wait_ge(weighted, h + 1)
                nc.scalar.activation(osq[:].rearrange("p t n -> p (t n)"), ps_o[:], ACT.Square).then_inc(o_squared, 1)
                act.wait_ge(o_mean, h + 1)
                nc.scalar.activation(o_std[:], o_ms[:], ACT.Sqrt).then_inc(o_rooted, 1)
                if not last:
                    copy_v(h + 1)
                else:
                    act.wait_ge(gate_summed, 1)
                    nc.scalar.activation(g.gate[:], ps_kv[:], ACT.Copy).then_inc(gate_done, 1)
                act.wait_ge(o_transposed, h + 1)
                nc.scalar.activation(oT[:, ds(h, 1), :].rearrange("p a n -> p (a n)"), ps_q[:], ACT.Copy,
                                     scale=g.subln[:]).then_inc(o_copied, 1)

            act.sem_inc(a_copied, 4)
            act.sem_inc(o_copied, 2)
            copy_v(0)
            with act.Fori(0, HEADS - 1) as h:
                head(h, False)
            head(HEADS - 1, True)

        @block.vector
        def _(dve):
            def rotate(h, chain, between=None):
                for i, (ps, dst) in enumerate(((ps_q, qT), (ps_k, kT))):
                    factor = HD ** -0.5 if i == 0 else 1.0
                    dve.wait_ge(qk_projected, 2 * h + 1 + i)
                    for q in range(4):
                        rows, other = slice(32 * q, 32 * q + 32), slice(32 * (q ^ 1), 32 * (q ^ 1) + 32)
                        nc.vector.scalar_tensor_tensor(rot[rows, :], ps[other, :], factor, g.sin[other, :],
                                                       ALU.mult, ALU.mult)
                    chain(nc.vector.scalar_tensor_tensor(rot2[:], ps[:], factor, g.cos[:], ALU.mult, ALU.mult))
                    nc.vector.tensor_tensor(dst[:], rot[:], rot2[:], ALU.add).then_inc(rotated, 1)
                    if between and i == 0:
                        between()
                    dve.wait_ge(rotated, 2 * h + 1 + i)

            def ada(h, chunks):
                for k in chunks:
                    if k == 0:
                        dve.wait_ge(partial_free, h + 1)
                    if k % ADA_HALF == 0:
                        dve.wait_ge(ada_loaded[k // ADA_HALF], 16 * h + 16)
                    add_ada(nc, g, dve, [k], ada_chain, h, ada_used, partial_done)

            def head(h, last):
                chain = Chain(dve, chain_s, 2 + HOPS * h)
                for u in range(8):
                    dve.wait_ge(scored, 8 * h + u + 1)
                    nc.vector.tensor_reduce(neg_max[:, u:u + 1], ps_s[u % 4][:], AX.X, ALU.max, negate=True)\
                        .then_inc(maxed, 1)
                dve.wait_ge(exped, 8 * h + 8)
                chain(nc.vector.reciprocal(inv_sum[:], row_sum[:]))
                chain(nc.vector.tensor_scalar(lam_inv[:], inv_sum[:], g.neg_lam[:], None, ALU.mult))
                for t in range(NT):
                    nc.vector.tensor_scalar(prob[:, 2 * t + 1, :], prob[:, 2 * t + 1, :], lam_inv[:, 2 * t + 1:2 * t + 2],
                                            None, ALU.mult).then_inc(chain_s, 1)
                    chain.n += 1
                for t in range(NT):
                    dve.wait_ge(chain_s, chain.base + 3 + t)
                    nc.vector.scalar_tensor_tensor(prob[:, 2 * t, :], prob[:, 2 * t, :], inv_sum[:, 2 * t:2 * t + 1],
                                                   prob[:, 2 * t + 1, :], ALU.mult, ALU.add).then_inc(mixed, 1)
                if not last:
                    rotate(h + 1, chain, lambda: ada(h, range(3)))
                dve.wait_ge(o_squared, h + 1)
                chain(nc.vector.reduce_sum(o_sum[:], osq[:], AX.X))
                nc.vector.tensor_scalar(o_ms[:], o_sum[:], 1.0 / P, EPS, ALU.mult, ALU.add).then_inc(o_mean, 1)
                dve.wait_ge(o_rooted, h + 1)
                chain(nc.vector.reciprocal(o_inv[:], o_std[:]))
                nc.vector.tensor_tensor(on[:], ps_o[:].rearrange("p (t n) -> p t n", n=P),
                                        o_inv[:].unsqueeze(2).to_broadcast([P, NT, P]), ALU.mult).then_inc(o_normed, 1)
                if not last:
                    ada(h, range(3, KC))
                assert chain.n == (HOPS - 2 if last else HOPS)

            dve.sem_inc(o_normed, 1)
            dve.sem_inc(ada_used, 2)
            rotate(0, Chain(dve, chain_s))
            with dve.Fori(0, HEADS - 1) as h:
                head(h, False)
            head(HEADS - 1, True)
            add_gated(nc, g, dve, chain_s, 2 + HOPS * HEADS - 2, projected_out, added,
                      [*ps_s, ps_k, ps_v, ps_o, ps_q], mix, (gate_done, 1))


def add_gated(nc, g, dve, chain_s, base, ready, added, banks, scratch, gate_ready=None):
    if gate_ready:
        dve.wait_ge(*gate_ready)
    for i, ps in enumerate(banks):
        t, n = divmod(i, 2)
        cols = slice(n * BANK, (n + 1) * BANK)
        dve.wait_ge(ready, i + 1)
        if i >= 2:
            dve.wait_ge(added, i - 1)
        nc.vector.tensor_tensor(scratch[:, i % 2, :], ps[:], g.gate[:, cols], ALU.mult).then_inc(chain_s, 1)
        dve.wait_ge(chain_s, base + i + 1)
        nc.vector.tensor_tensor(g.x[:, t, cols], g.x[:, t, cols], scratch[:, i % 2, :], ALU.add).then_inc(added, 1)


def experts(nc, g, layer):
    A = g.inputs
    tag = f"moe{layer}"
    with ExitStack() as scope:
        sb = lambda n, s, d=FP32: scope.enter_context(nc.sbuf_tensor(f"{tag}_{n}", s, d))
        ring_hi = sb("ring_hi", [P, 2, SLOT])
        slots = [g.ring[:, 0, :], g.ring[:, 1, :], ring_hi[:, 0, :], ring_hi[:, 1, :]]
        w_gate = [s[:, 0:KC * F].rearrange("p (k f) -> p k f", k=KC) for s in slots]
        w_up = [s[:, KC * F:2 * KC * F].rearrange("p (k f) -> p k f", k=KC) for s in slots]
        w_down = [s[:, 2 * KC * F:].rearrange("p (j n) -> p j n", j=2) for s in slots]
        w_router = sb("w_router", [P, KC, E])
        bias = sb("bias", [P, E])
        tile3 = [P, NT, E]
        score, select = sb("score", tile3), sb("select", tile3)
        top8 = sb("top8", [P, NT, EXPERT_GROUPS, 8])
        group_score = sb("group_score", [P, NT, EXPERT_GROUPS])
        above, equal = sb("above", [P, NT, 8, 8]), sb("equal", [P, NT, 8, 8])
        group_in, group_out = sb("group_in", [P, NT, 8]), sb("group_out", [P, NT, 8])
        top_sel = sb("top_sel", [P, NT, 8])
        greater, tied, chosen = sb("greater", tile3), sb("tied", tile3), sb("chosen", tile3)
        missing, weight_sum = sb("missing", [P, NT]), sb("weight_sum", [P, NT])
        place = sb("place", tile3)
        record = sb("record", [P, NT, E, 3])
        count_i = sb("count_i", [P, E + 1], I32)
        extra, done_before = sb("extra", [P, E]), sb("done_before", [P, E])
        over_f = sb("over_f", [P, 2])
        over_i = sb("over_i", [P, 2], I32)
        onehot = [sb(f"onehot{i}", [P, NT, P]) for i in range(2)]
        index = [sb(f"index{i}", [P, 2], I32) for i in range(RING)]
        weight = [sb(f"weight{i}", [P, 1]) for i in range(RING)]
        xg = [sb(f"xg{i}", [P, D]) for i in range(2)]
        xT = [sb(f"xT{i}", [P, KC, P]) for i in range(2)]
        weight_hi = [sb(f"weight_hi{i}", [P, 1]) for i in range(RING)]
        silu = sb("silu", [P, 2, P])
        hid_tok = sb("hid_tok", [P, F])
        hid = [sb(f"hid{i}", [P, 2, P]) for i in range(2)]
        out = [sb(f"out{i}", [P, D]) for i in range(2)]
        silu_all, hid_all = sb("silu_all", [P, 2, S]), sb("hid_all", [P, 2, S])
        total = sb("total", [P, 2, D])

        ps = lambda n, s: scope.enter_context(nc.psum_tensor(f"{tag}_{n}", s, FP32))
        ps_r, ps_p = ps("ps_r", [P, 8, E]), ps("ps_p", [P, 8, E])
        ps_i, ps_h = ps("ps_i", [P, BANK]), ps("ps_h", [P, 4, P])
        ps_x = [ps(f"ps_x{i}", [P, 4, P]) for i in range(2)]
        ps_y = [ps(f"ps_y{i}", [P, BANK]) for i in range(2)]
        ps_h_flat, silu_flat = ps_h[:].rearrange("p a b -> p (a b)"), silu[:].rearrange("p a b -> p (a b)")
        ps_turned = ps_h_flat[:, F:].rearrange("p (j n) -> p j n", j=2)
        LOW, HIGH = slice(0, NARROW), slice(P - NARROW, P)
        shared_banks = [ps_x[0][:].rearrange("p a b -> p (a b)"), ps_x[1][:].rearrange("p a b -> p (a b)"),
                        ps_y[0][:], ps_y[1][:]]

        sem = g.stage_semaphores(scope, f"{tag}_")
        router_loaded, routed, scored = sem("router_loaded"), sem("routed"), sem("scored")
        chain_s, chosen_done, placed, counts_done = sem("chain"), sem("chosen_done"), sem("placed"), sem("counts_done")
        over_done, over_stored, blanked = sem("over_done"), g.sem(f"over_stored{layer}"), sem("blanked")
        pool_turns = sem("pool_turns")
        shared_up, shared_silu, shared_hid = sem("shared_up"), sem("shared_silu"), sem("shared_hid")
        shared_down, shared_added = sem("shared_down"), sem("shared_added")
        loaded = g.expert_loaded[layer]
        onehot_done, looked_up, index_done = sem("onehot_done"), sem("looked_up"), sem("index_done")
        gathered = [g.sem(f"gathered{layer}_{i}") for i in range(2)]
        x_transposed, x_copied, up_done, silu_done = sem("x_transposed"), sem("x_copied"), sem("up_done"), sem("silu_done")
        hid_rows, hid_turned = sem("hid_rows"), sem("hid_turned")
        hid_done, down_done, out_lo, out_hi = sem("hid_done"), sem("down_done"), sem("out_lo"), sem("out_hi")
        scattered = [g.sem(f"scattered{layer}_{i}") for i in range(2)]
        over_scattered, over_free, all_scattered = g.sem(f"over_scattered{layer}"), sem("over_free"), sem("all_scattered")
        rows_loaded, row_chain, totalled = [sem(f"rows_loaded{i}") for i in range(2)], sem("row_chain"), sem("totalled")
        block = scope.enter_context(nc.Block())

        def passes(eng, step):
            for s in range(RING):
                step(0, s, False)
            with eng.Fori(1, E // RING - 1) as r:
                for s in range(RING):
                    step(r, s, False)
            for s in range(RING):
                step(E // RING - 1, s, True)

        def by_width(eng, n, wide_step, narrow_step):
            tokens = eng.value_load(count_i[0:1, ds(n, 1)], min_val=0, max_val=S)
            with eng.If(tokens > NARROW):
                wide_step()
            with eng.Else():
                narrow_step()

        def extra_passes(eng, step):
            eng.wait_ge(over_stored, 32)
            n_extra = eng.value_load(g.over_dram[P:P + 1, 0:1], min_val=0, max_val=MAX_OVERFLOW)
            with eng.Fori(0, MAX_OVERFLOW) as i:
                with eng.If(i < n_extra):
                    step(i)
                eng.nop()

        def extra_expert(eng, i):
            return eng.value_load(g.over_dram[ds(i, 1), 0:1], min_val=0, max_val=E - 1)

        @block.sync
        def _(sp):
            sp.dma_start(w_router[:], A["moe_w_router"][layer, :, :].rearrange("(p k) n -> p k n", k=KC)).then_inc(router_loaded, 16)
            sp.dma_start(bias[:], A["moe_router_bias"][layer, :].partition_broadcast(P)).then_inc(router_loaded, 16)
            for dst, name in ((w_gate[3], "moe_ws_gate"), (w_up[3], "moe_ws_up")):
                sp.dma_start(dst, A[name][layer, :, :].rearrange("(p k) f -> p k f", k=KC)).then_inc(loaded[3], 16)
            sp.dma_start(w_down[3], A["moe_ws_down"][layer, :, :].rearrange("(j p) n -> p j n", p=P)).then_inc(loaded[3], 16)

            def step(r, s, tail):
                n = RING * r + s
                if isinstance(r, int) and r == 0:
                    if s < 2:
                        return
                    if s == 3:
                        sp.wait_ge(shared_down, 8)
                else:
                    sp.wait_ge(down_done, n - (RING - 1))
                g.load_expert_into(sp, layer, slots[s], s, n)

            def extra_step(i):
                e = extra_expert(sp, i)
                sp.wait_ge(down_done, E + i)
                g.load_expert_into(sp, layer, slots[0], 0, e)

            passes(sp, step)
            extra_passes(sp, extra_step)
            sp.wait_ge(all_scattered, 1)
            for t in range(NT):
                if t >= 2:
                    sp.wait_ge(totalled, t - 1)
                sp.dma_start(slots[2 + t % 2], g.rows_dram[t * P * TOP_K:(t + 1) * P * TOP_K, :]
                             .rearrange("(p k) d -> p (k d)", k=TOP_K)).then_inc(rows_loaded[t % 2], 16)
            for i in range(2):
                sp.wait_ge(rows_loaded[i], 32)

        @block.gpsimd
        def _(pool):
            pool.sem_clear(g.other_semaphores)
            for i in range(2):
                pool.memset(xg[i][:], 0.0).then_inc(blanked, 1)
            pool.wait_ge(over_done, 1)
            pool.dma_start(g.over_dram[0:P, :], over_i[:]).then_inc(over_stored, 16)
            pool.dma_start(g.over_dram[P:P + 1, 0:1], count_i[0:1, E:E + 1]).then_inc(over_stored, 16)

            def wide(expert, move):
                tokens = pool.value_load(count_i[0:1, ds(expert, 1)], min_val=0, max_val=S)
                with pool.If(tokens > NARROW):
                    move(P)
                with pool.Else():
                    move(NARROW)

            def gather(n, s, expert):
                def move(rows):
                    pool.indirect_dma_start(out=xg[s % 2][0:rows, :], out_offset=None, in_=g.h_dram[:, :],
                                            in_offset=bass.IndirectOffsetOnAxis(ap=index[s][0:rows, 0:1], axis=0),
                                            bounds_check=S - 1, oob_is_err=False).then_inc(gathered[s % 2], 16)

                pool.wait_ge(index_done, n + 1)
                after(pool, x_transposed, n - 1)
                pool.sem_inc(pool_turns, 1)
                wide(expert, move)

            def scatter(n, s, expert, done):
                def move(rows):
                    pool.indirect_dma_start(out=g.rows_dram[:, :],
                                            out_offset=bass.IndirectOffsetOnAxis(ap=index[s][0:rows, 1:2], axis=0),
                                            in_=out[s % 2][0:rows, :], in_offset=None,
                                            bounds_check=S * TOP_K - 1, oob_is_err=False).then_inc(done, 16)

                pool.wait_ge(out_lo, n + 1)
                pool.wait_ge(out_hi, n + 1)
                pool.sem_inc(pool_turns, 1)
                wide(expert, move)

            def step(r, s, tail):
                n = RING * r + s
                if not tail or s < RING - 2:
                    gather(n + 2, (s + 2) % RING, n + 2)
                scatter(n, s, n, scattered[s % 2])

            def extra_step(i):
                e = extra_expert(pool, i)
                gather(E + i, 0, e)
                scatter(E + i, 0, e, over_scattered)
                pool.wait_ge(over_scattered, 16 * i + 16)
                pool.sem_inc(over_free, 1)

            pool.wait_ge(blanked, 2)
            gather(0, 0, 0)
            gather(1, 1, 1)
            passes(pool, step)
            for i in range(2):
                pool.wait_ge(scattered[i], 16 * E // 2)
            pool.sem_inc(over_free, 1)
            extra_passes(pool, extra_step)
            pool.sem_inc(all_scattered, 1)

        @block.tensor
        def _(pe):
            pe.wait_ge(router_loaded, 32)
            for t in range(NT):
                for k in range(KC):
                    last = nc.tensor.matmul(ps_r[:, t, :], g.hT[:, k, t * P:(t + 1) * P], w_router[:, k, :],
                                            start=(k == 0), stop=(k == KC - 1))
            last.then_inc(routed, 1)
            pe.wait_ge(loaded[3], 48)
            for i in range(4):
                w, j = (w_gate, w_up)[i // 2][3], i % 2
                for k in range(KC):
                    last = nc.tensor.matmul(shared_banks[i], w[:, k, j * P:(j + 1) * P], g.hT[:, k, :],
                                            start=(k == 0), stop=(k == KC - 1))
                last.then_inc(shared_up, 1)
            pe.wait_ge(chosen_done, 1)
            for t in range(NT + 1):
                for u in range(min(t + 1, NT)):
                    last = nc.tensor.matmul(ps_p[:, t, :], (g.tri if u == t else g.ones)[:], chosen[:, u, :],
                                            start=(u == 0), stop=(u == min(t, NT - 1)))
            last.then_inc(placed, 1)
            for i in range(8):
                t, n = divmod(i, 2)
                if i == 0:
                    pe.wait_ge(shared_hid, 2)
                if i >= 4:
                    pe.wait_ge(shared_added, i - 3)
                for j in range(2):
                    last = nc.tensor.matmul(shared_banks[i % 4], hid_all[:, j, t * P:(t + 1) * P],
                                            w_down[3][:, j, n * BANK:(n + 1) * BANK], start=(j == 0), stop=(j == 1))
                last.then_inc(shared_down, 1)
            pe.wait_ge(shared_added, 8)

            def look_up(n, s, expert):
                pe.wait_ge(onehot_done, n + 1)
                after(pe, index_done, n)
                for t in range(NT):
                    last = nc.tensor.matmul(ps_i[:, 0:3], onehot[s % 2][:, t, :],
                                            record[:, t, ds(expert, 1), :].rearrange("p a c -> p (a c)"),
                                            start=(t == 0), stop=(t == NT - 1))
                last.then_inc(looked_up, 1)

            def transpose_x(n, s, gathers):
                pe.wait_ge(gathered[s % 2], 16 * gathers)
                after(pe, x_copied, 2 * n)
                for k in range(KC):
                    last = nc.tensor.transpose(ps_x[k // 4][:, k % 4, :], xg[s % 2][:, k::KC], g.ident[:])
                last.then_inc(x_transposed, 1)

            def gate_up_ready(n, s, loads):
                pe.wait_ge(x_copied, 2 * n + 2)
                pe.wait_ge(loaded[s], 48 * loads)
                after(pe, hid_done, n)

            def gate_up(n, s):
                for i in range(4):
                    w, j = (w_gate, w_up)[i // 2][s], i % 2
                    for k in range(KC):
                        last = nc.tensor.matmul(ps_h[:, i, :], w[:, k, j * P:(j + 1) * P], xT[s % 2][:, k, :],
                                                start=(k == 0), stop=(k == KC - 1))
                last.then_inc(up_done, 1)

            def gate_up_narrow(n, s):
                for k in range(KC):
                    for w, rows in ((w_gate[s], LOW), (w_up[s], HIGH)):
                        last = nc.tensor.matmul(ps_h_flat[rows, 0:F], xT[s % 2][:, k, LOW], w[:, k, :],
                                                start=(k == 0), stop=(k == KC - 1))
                last.then_inc(up_done, 1)

            def turn_hidden(n):
                pe.wait_ge(hid_rows, n + 1)
                for j in range(2):
                    last = nc.tensor.transpose(ps_turned[:, j, :], hid_tok[:, j * P:(j + 1) * P], g.ident[:])
                last.then_inc(hid_turned, 1)

            def down_ready(n):
                pe.wait_ge(hid_done, n + 1)
                after(pe, out_lo, n)
                after(pe, out_hi, n)

            def down(n, s):
                down_ready(n)
                for i in range(2):
                    for j in range(2):
                        last = nc.tensor.matmul(ps_y[i][:], hid[s % 2][:, j, :], w_down[s][:, j, i * BANK:(i + 1) * BANK],
                                                start=(j == 0), stop=(j == 1))
                last.then_inc(down_done, 1)

            def down_narrow(n, s):
                down_ready(n)
                for j in range(2):
                    for i, rows in enumerate((LOW, HIGH)):
                        last = nc.tensor.matmul(ps_y[0][rows, :], hid[s % 2][:, j, LOW],
                                                w_down[s][:, j, i * BANK:(i + 1) * BANK], start=(j == 0), stop=(j == 1))
                last.then_inc(down_done, 1)

            def step(r, s, tail):
                n = RING * r + s

                def look_ahead():
                    if not tail or s < RING - 2:
                        look_up(n + 2, (s + 2) % RING, n + 2)

                def transpose_next():
                    if not tail or s < RING - 1:
                        transpose_x(n + 1, (s + 1) % RING, 2 * r + (s + 1) // 2 + 1)

                def wide_step():
                    gate_up(n, s)
                    look_ahead()
                    transpose_next()
                    down(n, s)
                    pe.sem_inc(hid_turned, 1)

                def narrow_step():
                    gate_up_narrow(n, s)
                    look_ahead()
                    turn_hidden(n)
                    transpose_next()
                    down_narrow(n, s)

                gate_up_ready(n, s, r + 1 + (s == 3))
                by_width(pe, n, wide_step, narrow_step)

            def extra_step(i):
                e = extra_expert(pe, i)
                look_up(E + i, 0, e)
                transpose_x(E + i, 0, E // 2 + 1 + i)
                gate_up_ready(E + i, 0, E // RING + 1 + i)
                gate_up(E + i, 0)
                down(E + i, 0)

            look_up(0, 0, 0)
            look_up(1, 1, 1)
            transpose_x(0, 0, 1)
            passes(pe, step)
            extra_passes(pe, extra_step)

        @block.scalar
        def _(act):
            act.wait_ge(routed, 1)
            nc.scalar.activation(score[:], ps_r[:, 0:NT, :], ACT.Sigmoid).then_inc(scored, 1)
            for j in range(2):
                act.wait_ge(shared_up, j + 1)
                nc.scalar.activation(silu_all[:, j, :], shared_banks[j], ACT.Silu).then_inc(shared_silu, 1)

            def copy_x(n, s):
                act.wait_ge(x_transposed, n + 1)
                after(act, up_done, n - 1)
                for half in range(2):
                    nc.scalar.activation(xT[s % 2][:, 4 * half:4 * half + 4, :], ps_x[half][:], ACT.Copy).then_inc(x_copied, 1)

            def silu_ready(n):
                act.wait_ge(up_done, n + 1)
                after(act, hid_done, n)

            def out_ready(n, s, scatters):
                act.wait_ge(down_done, n + 1)
                if scatters is not None:
                    after(act, scattered[s % 2], scatters)

            def silu_gate(n):
                silu_ready(n)
                nc.scalar.activation(silu[:], ps_h[:, 0:2, :], ACT.Silu).then_inc(silu_done, 1)

            def scale_out(n, s, scatters):
                out_ready(n, s, scatters)
                nc.scalar.activation(out[s % 2][:, 0:BANK], ps_y[0][:], ACT.Copy, scale=weight[s][:]).then_inc(out_lo, 1)

            def step(r, s, tail):
                n = RING * r + s

                def copy_next():
                    if not tail or s < RING - 1:
                        copy_x(n + 1, (s + 1) % RING)

                def wide_step():
                    silu_gate(n)
                    copy_next()
                    scale_out(n, s, 16 * (2 * r + s // 2))

                def narrow_step():
                    silu_ready(n)
                    nc.scalar.activation(silu_flat[HIGH, 0:F], ps_h_flat[LOW, 0:F], ACT.Silu).then_inc(silu_done, 1)
                    copy_next()
                    out_ready(n, s, 16 * (2 * r + s // 2))
                    nc.scalar.activation(out[s % 2][LOW, 0:BANK], ps_y[0][LOW, :], ACT.Copy, scale=weight[s][LOW, :])\
                        .then_inc(out_lo, 1)

                by_width(act, n, wide_step, narrow_step)

            def extra_step(i):
                copy_x(E + i, 0)
                silu_gate(E + i)
                scale_out(E + i, 0, None)

            copy_x(0, 0)
            passes(act, step)
            extra_passes(act, extra_step)

        @block.vector
        def _(dve):
            chain = Chain(dve, chain_s)
            tt, ts = nc.vector.tensor_tensor, nc.vector.tensor_scalar
            chain(nc.vector.memset(hid_tok[:], 0.0))
            dve.wait_ge(router_loaded, 32)
            dve.wait_ge(scored, 1)
            chain(tt(select[:], score[:], bias[:].unsqueeze(1).to_broadcast(tile3), ALU.add))
            for t in range(NT):
                for x in range(EXPERT_GROUPS):
                    last = nc.vector.max(top8[:, t, x, :], select[:, t, 8 * x:8 * x + 8])
            chain(last)
            chain(tt(group_score[:], top8[:, :, :, 0], top8[:, :, :, 1], ALU.add))
            pair = [P, NT, 8, 8]
            that, this = group_score[:].unsqueeze(2).to_broadcast(pair), group_score[:].unsqueeze(3).to_broadcast(pair)
            tt(above[:], that, this, ALU.is_gt)
            chain(tt(equal[:], that, this, ALU.is_equal))
            chain(tt(equal[:], equal[:], g.group_lower[:].unsqueeze(1).to_broadcast(pair), ALU.mult))
            chain(tt(above[:], above[:], equal[:], ALU.add))
            chain(nc.vector.reduce_sum(group_in[:], above[:], AX.X))
            chain(ts(group_in[:], group_in[:], float(TOPK_GROUPS), None, ALU.is_lt))
            chain(ts(group_out[:], group_in[:], 1e30, -1e30, ALU.mult, ALU.add))
            wide = lambda a: a[:].unsqueeze(3).to_broadcast(pair)
            split = lambda a: a[:].rearrange("p t (x e) -> p t x e", e=8)
            chain(tt(split(select), split(select), wide(group_in), ALU.mult))
            chain(tt(split(select), split(select), wide(group_out), ALU.add))
            for t in range(NT):
                last = nc.vector.max(top_sel[:, t, :], select[:, t, :])
            chain(last)
            sixth = top_sel[:, :, TOP_K - 1:TOP_K].to_broadcast(tile3)
            tt(greater[:], select[:], sixth, ALU.is_gt)
            chain(tt(g.prefix[:, 0, :, PAD:], select[:], sixth, ALU.is_equal))
            chain(nc.vector.reduce_sum(missing[:], greater[:], AX.X))
            chain(ts(missing[:], missing[:], -1.0, float(TOP_K), ALU.mult, ALU.add))

            def running_sum():
                for i in range(6):
                    a, b, shift = i % 2, (i + 1) % 2, 1 << i
                    chain(tt(g.prefix[:, b, :, PAD:], g.prefix[:, a, :, PAD:],
                             g.prefix[:, a, :, PAD - shift:PAD + E - shift], ALU.add))

            chain(nc.vector.tensor_copy(tied[:], g.prefix[:, 0, :, PAD:]))
            running_sum()
            chain(tt(g.prefix[:, 0, :, PAD:], g.prefix[:, 0, :, PAD:], tied[:], ALU.subtract))
            chain(tt(g.prefix[:, 0, :, PAD:], g.prefix[:, 0, :, PAD:], missing[:].unsqueeze(2).to_broadcast(tile3), ALU.is_lt))
            chain(tt(tied[:], tied[:], g.prefix[:, 0, :, PAD:], ALU.mult))
            tt(chosen[:], greater[:], tied[:], ALU.add).then_inc(chosen_done, 1)
            dve.wait_ge(chosen_done, 1)
            for j in range(2):
                dve.wait_ge(shared_silu, j + 1)
                dve.wait_ge(shared_up, j + 3)
                tt(hid_all[:, j, :], silu_all[:, j, :], shared_banks[2 + j], ALU.mult).then_inc(shared_hid, 1)
            chain(tt(score[:], score[:], chosen[:], ALU.mult))
            chain(nc.vector.reduce_sum(weight_sum[:], score[:], AX.X))
            chain(nc.vector.reciprocal(weight_sum[:], weight_sum[:]))
            chain(tt(score[:], score[:], weight_sum[:].unsqueeze(2).to_broadcast(tile3), ALU.mult))
            ts(record[:, :, :, 2], score[:], ROUTED_SCALE, None, ALU.mult)
            chain(nc.vector.tensor_copy(g.prefix[:, 0, :, PAD:], chosen[:]))
            running_sum()
            chain(tt(g.prefix[:, 0, :, PAD:], g.prefix[:, 0, :, PAD:], chosen[:], ALU.subtract))
            tt(record[:, :, :, 1], g.prefix[:, 0, :, PAD:], g.row_shift[:].unsqueeze(2).to_broadcast(tile3), ALU.add)
            nc.vector.tensor_copy(record[:, :, :, 0], g.tok_shift[:].unsqueeze(2).to_broadcast(tile3))
            dve.wait_ge(placed, 1)
            chain(nc.vector.scalar_tensor_tensor(place[:], ps_p[:, 0:NT, :], 1.0, chosen[:], ALU.add, ALU.mult))
            chain(ts(place[:], place[:], -1.0, None, ALU.add))
            counts = ps_p[:, NT, :]
            nc.vector.tensor_copy(count_i[:, 0:E], counts)
            chain(ts(extra[:], counts, float(SLOTS_PER_BLOCK), None, ALU.is_gt))
            for c in range(2, S // SLOTS_PER_BLOCK):
                chain(nc.vector.scalar_tensor_tensor(extra[:], counts, float(c * SLOTS_PER_BLOCK), extra[:], ALU.is_gt, ALU.add))
            chain(nc.vector.tensor_copy(g.prefix[:, 0, 0, PAD:], extra[:]))
            running_sum()
            ts(count_i[:, E:E + 1], g.prefix[:, 0, 0, PAD + E - 1:PAD + E], 0.0, None, ALU.add)
            chain(ts(done_before[:], g.prefix[:, 0, 0, PAD:], g.tok[:, 0:1], None, ALU.is_le))
            chain(nc.vector.reduce_sum(over_f[:, 0:1], done_before[:], AX.X))
            chain(tt(done_before[:], done_before[:], extra[:], ALU.mult))
            chain(nc.vector.reduce_sum(over_f[:, 1:2], done_before[:], AX.X))
            ts(over_i[:, 0:1], over_f[:, 0:1], float(E - 1), None, ALU.min)
            chain(tt(over_f[:, 1:2], g.tok[:, 0:1], over_f[:, 1:2], ALU.subtract))
            ts(over_i[:, 1:2], over_f[:, 1:2], 1.0, None, ALU.add).then_inc(over_done, 1)
            base = chain.n
            add_gated(nc, g, dve, chain_s, base, shared_down, shared_added, [shared_banks[i % 4] for i in range(8)],
                      total[:].rearrange("p a (b n) -> p (a b) n", n=BANK))
            chain.n += 8

            def one_hot(n, s, expert, places):
                after(dve, looked_up, n - 1)
                tt(onehot[s % 2][:], g.iota[:, places].unsqueeze(1).to_broadcast([P, NT, P]),
                   place[:, :, ds(expert, 1)].to_broadcast([P, NT, P]), ALU.is_equal).then_inc(onehot_done, 1)

            def indices(n, s, scatters):
                dve.wait_ge(looked_up, n + 1)
                if scatters is not None:
                    after(dve, scattered[s % 2], scatters)
                nc.vector.tensor_copy(weight[s][:], ps_i[:, 2:3])
                nc.vector.tensor_copy(weight_hi[s][HIGH, :], ps_i[LOW, 2:3])
                ts(index[s][:], ps_i[:, 0:2], SKIP, None, ALU.add).then_inc(index_done, 1)

            def hidden(n, s):
                dve.wait_ge(silu_done, n + 1)
                after(dve, down_done, n - 1)
                tt(hid[s % 2][:], silu[:], ps_h[:, 2:4, :], ALU.mult).then_inc(hid_done, 1)

            def out_ready(n, s, scatters):
                dve.wait_ge(down_done, n + 1)
                if scatters is not None:
                    after(dve, scattered[s % 2], scatters)

            def scale_out(n, s, scatters):
                out_ready(n, s, scatters)
                ts(out[s % 2][:, BANK:], ps_y[1][:], weight[s][:], None, ALU.mult).then_inc(out_hi, 1)

            def step(r, s, tail):
                n = RING * r + s

                def indices_ahead():
                    if not tail or s < RING - 2:
                        indices(n + 2, (s + 2) % RING, 16 * (2 * r + s // 2))

                def wide_step():
                    hidden(n, s)
                    dve.sem_inc(hid_rows, 1)
                    indices_ahead()
                    scale_out(n, s, 16 * (2 * r + s // 2))

                def narrow_step():
                    dve.wait_ge(silu_done, n + 1)
                    tt(hid_tok[LOW, :], silu_flat[HIGH, 0:F], ps_h_flat[HIGH, 0:F], ALU.mult).then_inc(hid_rows, 1)
                    indices_ahead()
                    dve.wait_ge(hid_turned, n + 1)
                    after(dve, down_done, n - 1)
                    nc.vector.tensor_copy(hid[s % 2][:, :, LOW], ps_turned[:, :, LOW]).then_inc(hid_done, 1)
                    out_ready(n, s, 16 * (2 * r + s // 2))
                    ts(out[s % 2][LOW, BANK:], ps_y[0][HIGH, :], weight_hi[s][HIGH, :], None, ALU.mult).then_inc(out_hi, 1)

                if not tail or s < RING - 3:
                    one_hot(n + 3, (s + 3) % RING, n + 3, slice(0, P))
                by_width(dve, n, wide_step, narrow_step)

            def extra_step(i):
                e = extra_expert(dve, i)
                block_of = dve.value_load(g.over_dram[ds(i, 1), 1:2], min_val=0, max_val=S // P - 1)
                one_hot(E + i, 0, e, ds(block_of * P, P))
                dve.wait_ge(over_free, i + 1)
                indices(E + i, 0, None)
                hidden(E + i, 0)
                scale_out(E + i, 0, None)

            one_hot(0, 0, 0, slice(0, P))
            one_hot(1, 1, 1, slice(0, P))
            indices(0, 0, 0)
            indices(1, 1, 0)
            one_hot(2, 2, 2, slice(0, P))
            passes(dve, step)
            extra_passes(dve, extra_step)
            for t in range(NT):
                dve.wait_ge(rows_loaded[t % 2], 16 * (t // 2 + 1))
                rows = slots[2 + t % 2].rearrange("p (k d) -> p k d", d=D)
                acc = total[:, t % 2, :]
                chain(tt(acc, rows[:, 0, :], rows[:, 1, :], ALU.add))
                for k in range(2, TOP_K - 1):
                    chain(tt(acc, acc, rows[:, k, :], ALU.add))
                tt(acc, acc, rows[:, TOP_K - 1, :], ALU.add).then_inc(totalled, 1)
                dve.wait_ge(totalled, t + 1)
                chain(tt(acc, acc, g.gate[:], ALU.mult))
                chain(tt(g.x[:, t, :], g.x[:, t, :], acc, ALU.add))


N_IN = 2 * SG_HALF // BANK
K_OUT = SG_HALF // P


def gating_buffers(nc, g, scope):
    ring = scope.enter_context(nc.sbuf_tensor("w_in_ring", [P, 2 * KC, BANK], FP32))
    b = Shared()
    b.ring, b.w_in = ring, [ring[:, i * KC:(i + 1) * KC, :] for i in range(2)]
    b.loaded = [g.sem(f"w_in_loaded{i}") for i in range(2)]
    return b


def load_w_in(g, b, eng, n, i):
    rows = g.inputs["sg_w_in"][0, :, :].rearrange("(p k) n -> p k n", k=KC)
    eng.dma_start(b.w_in[i], rows[:, :, ds(n * BANK, BANK)]).then_inc(b.loaded[i], 16)


def gating(nc, g, b):
    A = g.inputs
    with ExitStack() as scope:
        sb = lambda n, s, d=FP32: scope.enter_context(nc.sbuf_tensor(f"sg_{n}", s, d))
        z = sb("z", [P, NT, 2 * SG_HALF])
        usT = b.ring
        hT_flat = g.hT[:].rearrange("p k t -> p (k t)")
        ln_g, ln_b = hT_flat[:, 0:SG_HALF], hT_flat[:, SG_HALF:]
        w_s, w_sT = [sb(f"w_s{i}", [P, P]) for i in range(2)], [sb(f"w_sT{i}", [P, P]) for i in range(2)]
        b_s = sb("b_s", [P, GROUPS])
        us = [sb(f"us{i}", [P, NT, GROUP_DIM]) for i in range(2)]
        stats, moments = sb("stats", [P, NT, 4, 6]), sb("moments", [P, NT, 2])
        ln_var, ln_std, ln_inv = sb("ln_var", [P, NT]), sb("ln_std", [P, NT]), sb("ln_inv", [P, NT])
        mix = sb("mix", [P, 2, BANK])
        w_out = [z[:, c // 2, SG_HALF + (c % 2) * D:SG_HALF + (c % 2 + 1) * D] for c in range(8)]
        banks = scope.enter_context(nc.psum_tensor("sg_banks", [P, 8, BANK], FP32))
        ps_s = [banks[:, 2 * i:2 * i + 2, :].rearrange("p a (b c) -> p (a b) c", c=GROUP_DIM) for i in range(2)]
        ps_us, ps_w = banks[:, 4:6, :], banks[:, 6, 0:P]
        sem = g.stage_semaphores(scope, "sg_")
        z_ready, gelu_done, ln_loaded, bs_loaded = sem("z_ready"), sem("gelu_done"), sem("ln_loaded"), sem("bs_loaded")
        ws_loaded, ws_turned, ws_copied = [sem(f"ws_loaded{i}") for i in range(2)], sem("ws_turned"), sem("ws_copied")
        chain_s, var_done, std_done, scaled, shifted = sem("chain"), sem("var_done"), sem("std_done"), sem("scaled"), sem("shifted")
        spatial, gated, us_turned, us_copied = sem("spatial"), sem("gated"), sem("us_turned"), sem("us_copied")
        wo_loaded, wo_used, projected, added = [sem(f"wo_loaded{i}") for i in range(8)], sem("wo_used"), sem("projected"), sem("added")
        ada_loaded, ada_used, ada_chain = [sem(f"ada_loaded{i}") for i in range(2)], sem("ada_used"), sem("ada_chain")
        partial_done, partial_free, partial_stored = sem("partial_done"), sem("partial_free"), g.sem("partial_stored1")
        block = scope.enter_context(nc.Block())
        FIRST_ADA, ADA_ROWS = 9, 3
        LN_HOPS = 3

        @block.sync
        def _(sp):
            sp.dma_start(b_s[:], A["sg_b_s"][0, :, :]).then_inc(bs_loaded, 16)
            for i in range(2):
                sp.dma_start(w_s[i][:], A["sg_w_s"][0, i, :, :]).then_inc(ws_loaded[i], 16)
            assert ADA_ROWS == N_IN // 2 - 1
            with sp.Fori(1, N_IN // 2) as r:
                for half in range(2):
                    sp.wait_ge(ada_used, 2 * (r - 1) + half + 1)
                    load_ada(g, sp, FIRST_ADA + r - 1, half, ada_loaded[half])
                for i in range(2):
                    sp.wait_ge(z_ready, 4 * (2 * r + i - 1))
                    load_w_in(g, b, sp, 2 * r + i, i)
            sp.wait_ge(z_ready, 4 * N_IN)
            sp.dma_start(ln_g, A["sg_ln_g"][0, :].partition_broadcast(P)).then_inc(ln_loaded, 16)
            sp.dma_start(ln_b, A["sg_ln_b"][0, :].partition_broadcast(P)).then_inc(ln_loaded, 16)
            with sp.Fori(1, GROUPS // 2) as r:
                for i in range(2):
                    sp.wait_ge(ws_turned, 2 * r + i - 1)
                    sp.dma_start(w_s[i][:], A["sg_w_s"][0, ds(2 * r + i, 1), :, :].rearrange("a p q -> p (a q)"))\
                        .then_inc(ws_loaded[i], 16)
            for c in range(K_OUT):
                if c == 0:
                    sp.wait_ge(spatial, GROUPS)
                if c >= 8:
                    sp.wait_ge(wo_used, c - 7)
                sp.dma_start(w_out[c % 8], A["sg_w_out"][0, c * P:(c + 1) * P, :]).then_inc(wo_loaded[c % 8], 16)
            sp.wait_ge(ada_used, 2 * ADA_ROWS + 2)
            g.load_expert(sp, 1, 0, 0)
            g.load_expert(sp, 1, 1, 1)

        @block.gpsimd
        def _(pool):
            pool.sem_clear(g.other_semaphores)
            store_partials(g, pool, FIRST_ADA, ADA_ROWS, partial_done, partial_stored, partial_free)
            pool.wait_ge(ln_loaded, 32)
            with pool.Fori(0, GROUPS) as x:
                pool.wait_ge(scaled, x + 1)
                v = z[:, :, ds(SG_HALF + x * GROUP_DIM, GROUP_DIM)]
                nc.gpsimd.tensor_tensor(v, v, ln_b[:, ds(x * GROUP_DIM, GROUP_DIM)].unsqueeze(1)
                                        .to_broadcast([P, NT, GROUP_DIM]), ALU.add).then_inc(shifted, 1)

        @block.tensor
        def _(pe):
            with pe.Fori(0, N_IN // 2) as r:
                for i in range(2):
                    pe.wait_ge(b.loaded[i], 16 * r + 16)
                    for t in range(NT):
                        pe.wait_ge(gelu_done, 8 * r + 4 * i + t + 1)
                        for k in range(KC):
                            last = nc.tensor.matmul(banks[:, 4 * i + t, :], g.hT[:, k, t * P:(t + 1) * P], b.w_in[i][:, k, :],
                                                    start=(k == 0), stop=(k == KC - 1))
                        last.then_inc(z_ready, 1)

            def turn_w_s(x, i, loads):
                pe.wait_ge(ws_loaded[i], 16 * loads)
                after(pe, ws_copied, x)
                nc.tensor.transpose(ps_w, w_s[i][:], g.ident[:]).then_inc(ws_turned, 1)

            def mix_tokens(x, i):
                pe.wait_ge(shifted, x + 1)
                pe.wait_ge(ws_copied, x + 1)
                pe.wait_ge(gated, x + 1)
                for t in range(NT):
                    last = nc.tensor.matmul(ps_s[i][:, t, :], w_sT[i][:], z[:, t, ds(SG_HALF + x * GROUP_DIM, GROUP_DIM)],
                                            start=True, stop=True)
                last.then_inc(spatial, 1)

            def turn_us(x, i):
                pe.wait_ge(gated, x + 3)
                pe.wait_ge(us_copied, x + 1)
                for j in range(2):
                    for t in range(NT):
                        last = nc.tensor.transpose(ps_us[:, j, t * P:(t + 1) * P], us[i][:, t, j * P:(j + 1) * P], g.ident[:])
                last.then_inc(us_turned, 1)

            pe.sem_inc(us_turned, 2)
            pe.wait_ge(gelu_done, 8 + 4 * N_IN)
            turn_w_s(0, 0, 1)
            mix_tokens(0, 0)
            turn_w_s(1, 1, 1)
            with pe.Fori(0, GROUPS // 2 - 1) as r:
                for i in range(2):
                    mix_tokens(2 * r + 1 + i, (1 + i) % 2)
                    turn_w_s(2 * r + 2 + i, i, r + 2)
                    turn_us(2 * r + i, i)
            mix_tokens(GROUPS - 1, 1)
            turn_us(GROUPS - 2, 0)
            turn_us(GROUPS - 1, 1)
            pe.wait_ge(us_copied, GROUPS + 1)
            for c in range(K_OUT):
                pe.wait_ge(wo_loaded[c % 8], 16 * (c // 8 + 1))
                for i in range(8):
                    t, n = divmod(i, 2)
                    last = nc.tensor.matmul(banks[:, i, :], usT[:, c, t * P:(t + 1) * P], w_out[c % 8][:, n * BANK:(n + 1) * BANK],
                                            start=(c == 0), stop=(c == K_OUT - 1))
                    if c == K_OUT - 1:
                        last.then_inc(projected, 1)
                if c < K_OUT - 1:
                    last.then_inc(wo_used, 1)

        @block.scalar
        def _(act):
            act.sem_inc(gelu_done, 8)
            act.sem_inc(us_copied, 1)
            with act.Fori(0, N_IN // 2) as r:
                for i in range(2):
                    for t in range(NT):
                        act.wait_ge(z_ready, 8 * r + 4 * i + t + 1)
                        nc.scalar.activation(z[:, t, ds((2 * r + i) * BANK, BANK)], banks[:, 4 * i + t, :], ACT.Gelu)\
                            .then_inc(gelu_done, 1)
            act.wait_ge(var_done, 1)
            nc.scalar.activation(ln_std[:], ln_var[:], ACT.Sqrt).then_inc(std_done, 1)

            def copy_w_s(x, i):
                act.wait_ge(ws_turned, x + 1)
                after(act, spatial, x - 1)
                nc.scalar.activation(w_sT[i][:], ps_w, ACT.Copy).then_inc(ws_copied, 1)

            def copy_us(x):
                act.wait_ge(us_turned, x + 3)
                nc.scalar.activation(usT[:, ds(2 * x, 2), :], ps_us, ACT.Copy).then_inc(us_copied, 1)

            copy_w_s(0, 0)
            copy_w_s(1, 1)
            with act.Fori(0, GROUPS // 2 - 1) as r:
                for i in range(2):
                    copy_w_s(2 * r + 2 + i, i)
                    copy_us(2 * r + i)
            copy_us(GROUPS - 2)
            copy_us(GROUPS - 1)

        @block.vector
        def _(dve):
            chain = Chain(dve, chain_s)
            dve.sem_inc(gated, 2)
            dve.sem_inc(ada_used, 2)
            with dve.Fori(0, ADA_ROWS) as n:
                dve.wait_ge(partial_free, n + 1)
                for half in range(2):
                    dve.wait_ge(ada_loaded[half], 16 * n + 16)
                    add_ada(nc, g, dve, range(half * ADA_HALF, (half + 1) * ADA_HALF), ada_chain, n, ada_used, partial_done)
            for c in range(4):
                for t in range(NT):
                    dve.wait_ge(gelu_done, 8 + 4 * (4 + c) + t + 1)
                    last = nc.vector.bn_stats(stats[:, t, c, :], z[:, t, SG_HALF + c * BANK:SG_HALF + (c + 1) * BANK])
            chain(last)
            for t in range(NT):
                last = nc.vector.bn_aggr(moments[:, t, :], stats[:, t, :, :].rearrange("p a b -> p (a b)"))
            chain(last)
            nc.vector.tensor_scalar(ln_var[:], moments[:, :, 1], EPS, None, ALU.add).then_inc(var_done, 1)
            dve.wait_ge(std_done, 1)
            chain(nc.vector.reciprocal(ln_inv[:], ln_std[:]))
            dve.wait_ge(ln_loaded, 32)
            dve.wait_ge(bs_loaded, 16)

            def scale_v(x):
                group = Chain(dve, chain_s, LN_HOPS + x)
                for t in range(NT):
                    v = z[:, t, ds(SG_HALF + x * GROUP_DIM, GROUP_DIM)]
                    last = nc.vector.tensor_scalar(v, v, moments[:, t, 0:1], ln_inv[:, t:t + 1], ALU.subtract, ALU.mult)
                group(last)
                v = z[:, :, ds(SG_HALF + x * GROUP_DIM, GROUP_DIM)]
                nc.vector.tensor_tensor(v, v, ln_g[:, ds(x * GROUP_DIM, GROUP_DIM)].unsqueeze(1)
                                        .to_broadcast([P, NT, GROUP_DIM]), ALU.mult).then_inc(scaled, 1)

            def gate_u(x, i):
                dve.wait_ge(spatial, x + 1)
                dve.wait_ge(us_turned, x + 1)
                nc.vector.scalar_tensor_tensor(us[i][:], ps_s[i], b_s[:, ds(x, 1)], z[:, :, ds(x * GROUP_DIM, GROUP_DIM)],
                                               ALU.add, ALU.mult).then_inc(gated, 1)

            assert chain.n == LN_HOPS
            scale_v(0)
            scale_v(1)
            with dve.Fori(0, GROUPS // 2 - 1) as r:
                for i in range(2):
                    gate_u(2 * r + i, i)
                    scale_v(2 * r + 2 + i)
            gate_u(GROUPS - 2, 0)
            gate_u(GROUPS - 1, 1)
            add_gated(nc, g, dve, chain_s, LN_HOPS + GROUPS, projected, added, [banks[:, i, :] for i in range(8)], mix)


def final_norm(nc, g, out):
    with ExitStack() as scope:
        sb = lambda n, s, d=FP32: scope.enter_context(nc.sbuf_tensor(f"fin_{n}", s, d))
        gain, squares, y = sb("gain", [P, D]), sb("squares", [P, D]), sb("y", [P, NT, D])
        sums, mean_sq, std, rstd = sb("sums", [P, NT]), sb("mean_sq", [P, NT]), sb("std", [P, NT]), sb("rstd", [P, NT])
        sem = g.stage_semaphores(scope, "fin_")
        gain_loaded, squared, mean_done, std_done = sem("gain_loaded"), sem("squared"), sem("mean_done"), sem("std_done")
        inverted, normed, stored = sem("inverted"), sem("normed"), sem("stored")
        block = scope.enter_context(nc.Block())

        @block.gpsimd
        def _(pool):
            pool.sem_clear(g.other_semaphores)

        @block.sync
        def _(sp):
            sp.dma_start(gain[:], g.inputs["final_g"].partition_broadcast(P)).then_inc(gain_loaded, 16)
            for t in range(NT):
                sp.wait_ge(normed, t + 1)
                sp.dma_start(out[0, t * P:(t + 1) * P, :], y[:, t, :]).then_inc(stored, 16)
            sp.wait_ge(stored, 16 * NT)

        @block.scalar
        def _(act):
            for t in range(NT):
                nc.scalar.activation(squares[:], g.x[:, t, :], ACT.Square, accum_out=sums[:, t:t + 1]).then_inc(squared, 1)
                act.wait_ge(squared, t + 1)
            act.wait_ge(mean_done, 1)
            nc.scalar.activation(std[:], mean_sq[:], ACT.Sqrt).then_inc(std_done, 1)

        @block.vector
        def _(dve):
            dve.wait_ge(squared, NT)
            nc.vector.tensor_scalar(mean_sq[:], sums[:], 1.0 / D, EPS, ALU.mult, ALU.add).then_inc(mean_done, 1)
            dve.wait_ge(std_done, 1)
            nc.vector.reciprocal(rstd[:], std[:]).then_inc(inverted, 1)
            dve.wait_ge(inverted, 1)
            dve.wait_ge(gain_loaded, 16)
            for t in range(NT):
                nc.vector.scalar_tensor_tensor(y[:, t, :], g.x[:, t, :], rstd[:, t:t + 1], gain[:], ALU.mult, ALU.mult)\
                    .then_inc(normed, 1)


def build(nc, inputs, out):
    g = Shared()
    g.inputs = inputs
    g.sems = ExitStack()
    with g.sems, ExitStack() as persistent:
        carried = {n: g.sems.enter_context(nc.semaphore(n)) for n in
                   ["q_loaded", "k_loaded", "v_loaded", "wo_loaded", "w_in_loaded0", "w_in_loaded1"] +
                   ["small_loaded", "partial_stored0", "partial_stored1"] +
                   [f"expert_loaded{layer}_{s}" for layer in range(2) for s in range(RING)] +
                   [n.format(layer) for layer in range(2) for n in
                    ("h_stored{}_0", "h_stored{}_1", "over_stored{}", "gathered{}_0", "gathered{}_1", "scattered{}_0", "scattered{}_1",
                     "over_scattered{}")]}
        g.sem = lambda n: carried[n]
        sb = lambda n, s, d=FP32: persistent.enter_context(nc.sbuf_tensor(n, s, d))
        g.x, g.hT, g.gate = sb("x", [P, NT, D]), sb("hT", [P, KC, S]), sb("gate", [P, D])
        g.ring = sb("ring", [P, 2, SLOT])
        g.cond, g.partial = sb("cond", [P, KC]), sb("partial", [P, D])
        g.ident, g.tri, g.ones = sb("ident", [P, P]), sb("tri", [P, P]), sb("ones", [P, P])
        g.group_lower = sb("group_lower", [P, EXPERT_GROUPS, EXPERT_GROUPS])
        g.iota = sb("iota", [P, S])
        g.tok_i = sb("tok_i", [P, NT], I32)
        g.tok, g.tok_shift, g.row_shift = sb("tok", [P, NT]), sb("tok_shift", [P, NT]), sb("row_shift", [P, NT])
        g.prefix = sb("prefix", [P, 2, NT, PAD + E])
        g.mod_dram = nc.dram_tensor("mod_dram", (12, P, D), FP32).ap()
        g.h_dram = nc.dram_tensor("h_dram", (S, D), FP32).ap()
        g.rows_dram = nc.dram_tensor("rows_dram", (S * TOP_K, D), FP32).ap()
        g.over_dram = nc.dram_tensor("over_dram", (P + 1, 2), I32).ap()
        g.expert_loaded = [[g.sem(f"expert_loaded{layer}_{s}") for s in range(RING)] for layer in range(2)]

        def load_expert_into(eng, layer, slot, s, e):
            third = KC * F
            for i, name in enumerate(("moe_w_gate", "moe_w_up")):
                eng.dma_start(slot[:, i * third:(i + 1) * third].rearrange("p (k f) -> p k f", k=KC),
                              inputs[name][layer, ds(e, 1), :, :].rearrange("a (p k) f -> p (a k) f", k=KC))\
                    .then_inc(g.expert_loaded[layer][s], 16)
            eng.dma_start(slot[:, 2 * third:].rearrange("p (j n) -> p j n", j=2),
                          inputs["moe_w_down"][layer, ds(e, 1), :, :].rearrange("a (j p) n -> p (a j) n", p=P))\
                .then_inc(g.expert_loaded[layer][s], 16)

        g.load_expert_into = load_expert_into

        numbers = sorted(nc.free_semaphores)
        half = len(numbers) // 2
        assert numbers[2 * half - 1] - numbers[0] == 2 * half - 1
        sets = [range(numbers[i * half], numbers[i * half] + half) for i in range(2)]
        g.stage = 0

        def stage_semaphores(scope, prefix):
            mine, g.other_semaphores = sets[g.stage % 2], sets[(g.stage + 1) % 2]
            g.stage += 1
            left = iter(mine)
            return lambda n: scope.enter_context(nc.semaphore(prefix + n, num=next(left)))

        g.stage_semaphores = stage_semaphores
        g.load_expert = lambda eng, layer, s, e: load_expert_into(eng, layer, g.ring[:, s, :], s, e)

        with ExitStack() as rope:
            g.cos, g.sin, g.subln, g.neg_lam = (rope.enter_context(nc.sbuf_tensor(n, [P, w], FP32))
                                                for n, w in (("cos", S), ("sin", S), ("subln", 1), ("neg_lam", 1)))
            conditioning(nc, g)
            with ExitStack() as buffers:
                b = attention_buffers(nc, g, buffers)
                normalise(nc, g, "n0a", 0, 0, 2, False, lambda sp: [load_head(g, b, sp, 0, i) for i in range(3)])
                attention(nc, g, b)
        normalise(nc, g, "n0b", 0, 1, 3, True, lambda sp: None)
        experts(nc, g, 0)
        with ExitStack() as buffers:
            b = gating_buffers(nc, g, buffers)
            normalise(nc, g, "n1a", 1, 0, 3, False, lambda sp: [load_w_in(g, b, sp, i, i) for i in range(2)])
            gating(nc, g, b)
        normalise(nc, g, "n1b", 1, 1, 3, True, lambda sp: None)
        experts(nc, g, 1)
        final_norm(nc, g, out)


_INS = ["x", "c", "positions", "norm1_g", "norm2_g", "ada_w", "ada_b", "da_w_in", "da_lam_q1", "da_lam_k1",
        "da_lam_q2", "da_lam_k2", "da_subln_g", "da_w_out", "sg_w_in", "sg_ln_g", "sg_ln_b", "sg_w_s", "sg_b_s",
        "sg_w_out", "moe_w_router", "moe_router_bias", "moe_w_gate", "moe_w_up", "moe_w_down", "moe_ws_gate",
        "moe_ws_up", "moe_ws_down", "final_g"]


def kernel(**inputs):
    import numpy as np
    import concourse.bacc as bacc
    from concourse import mybir as mb
    from concourse.bass_utils import run_bass_kernel_spmd as run

    nc = bacc.Bacc("TRN2", target_bir_lowering=False, num_devices=1)
    arrays = {name: np.ascontiguousarray(inputs[name]) for name in _INS}
    freq = np.float32(THETA) ** (-np.arange(0, HD, 2, dtype=np.float32) / np.float32(HD))
    arrays["rope_inv_freq"] = np.ascontiguousarray(np.tile(freq.astype(np.float32), 4)[:, None])
    arrays["sg_b_s"] = np.ascontiguousarray(np.swapaxes(arrays["sg_b_s"], 1, 2))
    arrays["ada_w"] = np.ascontiguousarray(np.swapaxes(arrays["ada_w"].reshape(2, D, 6, D), 1, 2).reshape(12, D, D))
    aps = {name: nc.dram_tensor(f"in_{name}", a.shape, mb.dt.from_np(a.dtype), kind="ExternalInput").ap()
           for name, a in arrays.items()}
    out = nc.dram_tensor("out_0", (1, S, D), FP32, kind="ExternalOutput").ap()
    build(nc, aps, out)
    result = run(nc, [{f"in_{name}": a for name, a in arrays.items()}], core_ids=[0])
    return result.results[0]["out_0"]
```

```python
import math
from contextlib import ExitStack

import concourse.bass as bass
from concourse import mybir

FP32 = mybir.dt.float32
I32 = mybir.dt.int32
ALU = mybir.AluOpType
ACT = mybir.ActivationFunctionType
AX = mybir.AxisListType

P = 128
D = 1024
S = 512
NT = S // P
KC = D // P
EPS = 1e-6
BANK = 512

HEADS = 8
HD = 64
LAMBDA_INIT = 0.8 - 0.6 * math.exp(-0.3 * 0)
THETA = 10000.0

SG_HALF = 2 * D
GROUPS = 8
GROUP_DIM = SG_HALF // GROUPS

E = 64
F = D // 4
TOP_K = 6
EXPERT_GROUPS = 8
TOPK_GROUPS = 4
ROUTED_SCALE = 2.5
RING = 4
SLOT = 3 * KC * F
SLOTS_PER_BLOCK = P
NARROW = 64
MAX_OVERFLOW = S * TOP_K // SLOTS_PER_BLOCK
OVERFLOW_GROUP = 4
ROW_STEP = 16
PAD = 32
SKIP = 4096.0


class Shared:
    pass


def ds(start, size):
    return bass.ds(start, size)


def after(engine, semaphore, count):
    if not (isinstance(count, int) and count <= 0):
        engine.wait_ge(semaphore, count)


class Chain:

    def __init__(self, engine, semaphore, base=0):
        self.engine, self.semaphore, self.base, self.n = engine, semaphore, base, 0

    def __call__(self, instruction):
        instruction.then_inc(self.semaphore, 1)
        self.n += 1
        self.engine.wait_ge(self.semaphore, self.base + self.n)


ADA_HALF = KC // 2


def ada_buffer(g, half):
    return g.ring[:, half, 0:ADA_HALF * D].rearrange("p (k n) -> p k n", n=D)


def load_ada(g, eng, n, half, loaded):
    rows = g.inputs["ada_w"][ds(n, 1), :, :].rearrange("a (p k) n -> p (a k) n", k=KC)
    eng.dma_start(ada_buffer(g, half), rows[:, half * ADA_HALF:(half + 1) * ADA_HALF, :]).then_inc(loaded, 16)


def feature_modulation(nc, g, chain, ps, bias_T, gain_T):
    nc.vector.tensor_tensor(g.shift_T[:], ps[:, 0, :], bias_T[:, 0, :], ALU.add)
    chain(nc.vector.tensor_tensor(g.scale_T[:], ps[:, 1, :], bias_T[:, 1, :], ALU.add))
    return nc.vector.scalar_tensor_tensor(g.scale_T[:], g.scale_T[:], 1.0, gain_T[:], ALU.add, ALU.mult)


def add_chunk(nc, g, dve, partial, w, k, chain_s, count):
    if k:
        dve.wait_ge(chain_s, KC * count + k)
        op = nc.vector.scalar_tensor_tensor(partial, w, g.cond[:, k:k + 1], partial, ALU.mult, ALU.add)
    else:
        op = nc.vector.tensor_scalar(partial, w, g.cond[:, 0:1], None, ALU.mult)
    return op.then_inc(chain_s, 1)


def sum_feature_major(nc, g, ps, partial):
    for k in range(KC):
        last = nc.tensor.matmul(ps[:, k:k + 1], partial[:, k::KC], g.ones[:, 0:1], start=True, stop=True)
    return last


def add_ada(nc, g, dve, chunks, chain_s, count, last_of_half, last_of_row):
    for k in chunks:
        add_chunk(nc, g, dve, g.partial[:], ada_buffer(g, k // ADA_HALF)[:, k % ADA_HALF, :], k, chain_s, count)
        if k % ADA_HALF == ADA_HALF - 1:
            dve.wait_ge(chain_s, KC * count + k + 1)
            dve.sem_inc(last_of_half, 1)
        if k == KC - 1:
            dve.sem_inc(last_of_row, 1)


def conditioning(nc, g):
    A = g.inputs
    with ExitStack() as scope:
        sb = lambda n, s, d=FP32: scope.enter_context(nc.sbuf_tensor(n, s, d))
        ada_row1, partial1 = sb("ada_row1", [P, KC, D]), sb("partial1", [P, D])
        gain_T, bias_T = sb("gain_T", [P, KC]), sb("bias_T", [P, 2, KC])
        ps_T = scope.enter_context(nc.psum_tensor("ps_T", [P, 2, KC], FP32))
        c_cols = sb("c_cols", [P, KC])
        pos_i = sb("pos_i", [P, S], I32)
        pos_f = sb("pos_f", [P, S])
        angle = sb("angle", [P, S])
        turns = sb("turns", [P, S])
        inv_freq = sb("inv_freq", [P, 1])
        half_pi = sb("half_pi", [P, 1])
        lam_in = sb("lam_in", [P, 4, HD])
        lam_prod = sb("lam_prod", [P, 2, HD])
        lam_sum = sb("lam_sum", [P, 2])
        lam_exp = sb("lam_exp", [P, 2])
        iota_i = sb("iota_i", [P, S], I32)
        sem = g.stage_semaphores(scope, "")
        c_loaded, cond_done = sem("c_loaded"), sem("cond_done")
        ada_loaded = [sem(f"ada_loaded{i}") for i in range(2)]
        row1_loaded, ada_chain, rows_summed, small_rows_loaded = [sem(f"row1_loaded{i}") for i in range(2)], sem("ada_chain"), sem("rows_summed"), sem("small_rows_loaded")
        g.squared = sem("squared")
        small_loaded, consts_built, iota_built = g.sem("small_loaded"), sem("consts_built"), sem("iota_built")
        chain_s, angle_done, abs_done, trig_done = sem("dve_chain0"), sem("angle_done"), sem("abs_done"), sem("trig_done")
        lam_summed, lam_exped = sem("lam_summed"), sem("lam_exped")
        x_loaded = sem("x_loaded")
        block = scope.enter_context(nc.Block())

        @block.sync
        def _(sp):
            sp.dma_start(c_cols[:], A["c"].rearrange("a (p k) -> p (a k)", k=KC)).then_inc(c_loaded, 16)
            for half in range(2):
                load_ada(g, sp, 0, half, ada_loaded[half])
            sp.dma_start(bias_T[:], A["ada_b"][0, 0:2 * D].rearrange("(i p k) -> p i k", i=2, k=KC)).then_inc(small_rows_loaded, 16)
            sp.dma_start(gain_T[:], A["norm1_g"][0, :].rearrange("(p k) -> p k", k=KC)).then_inc(small_rows_loaded, 16)
            row1 = A["ada_w"][1, :, :].rearrange("(p k) n -> p k n", k=KC)
            for half in range(2):
                ks = slice(half * ADA_HALF, (half + 1) * ADA_HALF)
                sp.dma_start(ada_row1[:, ks, :], row1[:, ks, :]).then_inc(row1_loaded[half], 16)
            sp.dma_start(g.x[:, :, :], A["x"][0, :, :].rearrange("(t p) d -> p t d", p=P)).then_inc(x_loaded, 16)
            sp.wait_ge(x_loaded, 16)

        @block.gpsimd
        def _(pool):
            pool.sem_clear(g.other_semaphores)
            pool.dma_start(pos_i[:], A["positions"][0, :].partition_broadcast(P)).then_inc(small_loaded, 16)
            pool.dma_start(inv_freq[:], A["rope_inv_freq"]).then_inc(small_loaded, 16)
            for i, name in enumerate(("da_lam_q1", "da_lam_k1", "da_lam_q2", "da_lam_k2")):
                pool.dma_start(lam_in[:, i, :], A[name][0, :].partition_broadcast(P)).then_inc(small_loaded, 16)
            pool.dma_start(g.subln[:], A["da_subln_g"].rearrange("a p -> p a")).then_inc(small_loaded, 16)
            pool.memset(g.ident[:], 0.0).then_inc(consts_built, 1)
            pool.memset(g.tri[:], 1.0).then_inc(consts_built, 1)
            pool.memset(g.group_lower[:], 1.0).then_inc(consts_built, 1)
            pool.wait_ge(consts_built, 3)
            pool.affine_select(out=g.ident[:], in_=g.ident[:], compare_op=ALU.not_equal, fill=1.0, base=0,
                               pattern=[[-1, P]], channel_multiplier=1).then_inc(consts_built, 1)
            pool.affine_select(out=g.tri[:], in_=g.tri[:], compare_op=ALU.is_gt, fill=0.0, base=0,
                               pattern=[[1, P]], channel_multiplier=-1).then_inc(consts_built, 1)
            pool.affine_select(out=g.group_lower[:], in_=g.group_lower[:], compare_op=ALU.is_gt, fill=0.0, base=0,
                               pattern=[[1, EXPERT_GROUPS], [-1, EXPERT_GROUPS]], channel_multiplier=0)\
                .then_inc(consts_built, 1)
            pool.memset(g.ones[:], 1.0).then_inc(consts_built, 1)
            pool.iota(iota_i[:], pattern=[[1, S]], base=0, channel_multiplier=0).then_inc(iota_built, 1)
            pool.iota(g.tok_i[:], pattern=[[P, NT]], base=0, channel_multiplier=1).then_inc(iota_built, 1)

        @block.scalar
        def _(act):
            act.wait_ge(c_loaded, 16)
            nc.scalar.activation(g.cond[:], c_cols[:], ACT.Silu).then_inc(cond_done, 1)
            act.wait_ge(x_loaded, 16)
            square_tiles(nc, g, act, x_loaded, 0)
            act.wait_ge(lam_summed, 1)
            nc.scalar.activation(lam_exp[:], lam_sum[:], ACT.Exp).then_inc(lam_exped, 1)
            act.wait_ge(angle_done, 1)
            nc.scalar.activation(turns[:], angle[:], ACT.Abs).then_inc(abs_done, 1)
            act.wait_ge(abs_done, 1)
            nc.scalar.activation(g.cos[:], turns[:], ACT.Sin, bias=half_pi[:], scale=-1.0).then_inc(trig_done, 1)
            for q in range(4):
                rows = slice(32 * q, 32 * q + 32)
                nc.scalar.activation(g.sin[rows, :], angle[rows, :], ACT.Sin, scale=-1.0 if q % 2 else 1.0)\
                    .then_inc(trig_done, 1)

        @block.tensor
        def _(pe):
            pe.wait_ge(consts_built, 7)
            for row, partial in enumerate((g.partial, partial1)):
                pe.wait_ge(ada_chain, KC * (row + 1))
                sum_feature_major(nc, g, ps_T[:, row, :], partial).then_inc(rows_summed, 1)

        @block.vector
        def _(dve):
            chain = Chain(dve, chain_s)
            dve.wait_ge(cond_done, 1)
            for k in range(KC):
                if k % ADA_HALF == 0:
                    dve.wait_ge(ada_loaded[k // ADA_HALF], 16)
                add_chunk(nc, g, dve, g.partial[:], ada_buffer(g, k // ADA_HALF)[:, k % ADA_HALF, :], k, ada_chain, 0)
            for k in range(KC):
                if k % ADA_HALF == 0:
                    dve.wait_ge(row1_loaded[k // ADA_HALF], 16)
                add_chunk(nc, g, dve, partial1[:], ada_row1[:, k, :], k, ada_chain, 1)
            dve.wait_ge(small_loaded, 7 * 16)
            chain(nc.vector.tensor_tensor(lam_prod[:], lam_in[:, 0:4:2, :], lam_in[:, 1:4:2, :], ALU.mult))
            nc.vector.reduce_sum(lam_sum[:], lam_prod[:], AX.X).then_inc(lam_summed, 1)
            nc.vector.memset(half_pi[:], math.pi / 2)
            chain(nc.vector.tensor_copy(pos_f[:], pos_i[:]))
            chain(nc.vector.tensor_scalar(angle[:], pos_f[:], inv_freq[:], None, ALU.mult))
            magic = 1.5 * 2.0 ** 23
            chain(nc.vector.tensor_scalar(turns[:], angle[:], 1.0 / (2 * math.pi), magic, ALU.mult, ALU.add))
            chain(nc.vector.tensor_scalar(turns[:], turns[:], -magic, None, ALU.add))
            first = 6.28125
            second = math.floor((2 * math.pi - first) * 2 ** 22) / 2 ** 22
            third = 2 * math.pi - first - second
            for part in (first, second, third):
                chain(nc.vector.scalar_tensor_tensor(angle[:], turns[:], -part, angle[:], ALU.mult, ALU.add))
            nc.vector.tensor_scalar(angle[:], angle[:], 3.1415925, -3.1415925, ALU.min, ALU.max).then_inc(angle_done, 1)
            dve.wait_ge(iota_built, 2)
            nc.vector.tensor_copy(g.iota[:], iota_i[:])
            chain(nc.vector.tensor_copy(g.tok[:], g.tok_i[:]))
            nc.vector.tensor_scalar(g.tok_shift[:], g.tok[:], -SKIP, None, ALU.add)
            nc.vector.tensor_scalar(g.row_shift[:], g.tok[:], float(TOP_K), -SKIP, ALU.mult, ALU.add)
            nc.vector.tensor_scalar(g.subln[:], g.subln[:], 1.0 - LAMBDA_INIT, None, ALU.mult)
            nc.vector.memset(g.prefix[:], 0.0)
            dve.wait_ge(lam_exped, 1)
            chain(nc.vector.tensor_tensor(g.neg_lam[:], lam_exp[:, 1:2], lam_exp[:, 0:1], ALU.subtract))
            chain(nc.vector.tensor_scalar(g.neg_lam[:], g.neg_lam[:], -LAMBDA_INIT, None, ALU.add))
            dve.wait_ge(rows_summed, 2)
            dve.wait_ge(small_rows_loaded, 32)
            feature_modulation(nc, g, chain, ps_T, bias_T, gain_T)


def square_tiles(nc, g, act, ready, per_tile):
    for t in range(NT):
        after(act, ready, per_tile * (t + 1))
        nc.scalar.activation(g.squares[:], g.x[:, t, :], ACT.Square, accum_out=g.sums[:, t:t + 1]).then_inc(g.squared, 1)
        act.wait_ge(g.squared, t + 1)


def store_partials(g, pool, first, rows, done, stored, free):
    pool.sem_inc(free, 1)
    with pool.Fori(0, rows) as n:
        pool.wait_ge(done, n + 1)
        pool.dma_start(g.mod_dram[ds(first + n, 1), :, :].rearrange("a p n -> p (a n)"), g.partial[:]).then_inc(stored, 16)
        pool.wait_ge(stored, 16 * n + 16)
        pool.sem_inc(free, 1)


def sum_conditioning(nc, g, partial, ada_b, ps):
    for n in range(D // BANK):
        cols = slice(n * BANK, (n + 1) * BANK)
        last = nc.tensor.matmul(ps[:, cols], g.ones[:], partial[:, cols], start=True, stop=ada_b is None)
        if ada_b is not None:
            last = nc.tensor.matmul(ps[:, cols], g.ones[0:1, :], ada_b[:, cols], start=False, stop=True)
    return last


def normalise(nc, g, tag, layer, which, xn, load_ahead):
    A = g.inputs
    norm_g = A["norm1_g" if which == 0 else "norm2_g"][layer, :]
    first_row = 6 * layer + 3 * which
    with ExitStack() as scope:
        sb = lambda n, s, d=FP32: scope.enter_context(nc.sbuf_tensor(f"{tag}_{n}", s, d))
        partial = sb("partial", [P, 2, D])
        gain_T, bias_T = sb("gain_T", [P, KC]), sb("bias_T", [P, 2, KC])
        mean_sq, std, rstd = sb("mean_sq", [P, NT]), sb("std", [P, NT]), sb("rstd", [P, NT])
        ps_t = scope.enter_context(nc.psum_tensor(f"{tag}_ps", [P, KC, BANK], FP32))
        ps_T = ps_t[:, KC - 1, 0:2 * KC].rearrange("p (i k) -> p i k", i=2)
        sem = g.stage_semaphores(scope, f"{tag}_")
        small_loaded, partial_loaded = sem("small_loaded"), [sem(f"partial_loaded{i}") for i in range(2)]
        mean_done, std_done, xn_done, rows_summed = sem("mean_done"), sem("std_done"), sem("xn_done"), sem("rows_summed")
        chain_s, modulation_ready, transposed = sem("chain"), sem("modulation_ready"), sem("transposed")
        block = scope.enter_context(nc.Block())

        @block.sync
        def _(sp):
            if first_row:
                sp.dma_start(bias_T[:], A["ada_b"][layer, 3 * which * D:(3 * which + 2) * D]
                             .rearrange("(i p k) -> p i k", i=2, k=KC)).then_inc(small_loaded, 16)
                sp.dma_start(gain_T[:], norm_g.rearrange("(p k) -> p k", k=KC)).then_inc(small_loaded, 16)
                for i in range(2):
                    sp.dma_start(partial[:, i, :], g.mod_dram[first_row + i, :, :]).then_inc(partial_loaded[i], 16)
            load_ahead(sp)

        @block.gpsimd
        def _(pool):
            pool.sem_clear(g.other_semaphores)

        @block.scalar
        def _(act):
            act.wait_ge(mean_done, 1)
            nc.scalar.activation(std[:], mean_sq[:], ACT.Sqrt).then_inc(std_done, 1)
            if first_row:
                act.wait_ge(modulation_ready, 1)
            for k in range(0, KC, 2):
                act.wait_ge(transposed, k + 1)
                nc.scalar.activation(g.hT[:, k, :], ps_t[:, k, :], ACT.Identity, scale=g.scale_T[:, k:k + 1],
                                     bias=g.shift_T[:, k:k + 1])

        @block.tensor
        def _(pe):
            def transpose(t, k):
                return nc.tensor.transpose(ps_t[:, k, t * P:(t + 1) * P], xn[t][:, k::KC], g.ident[:])

            for t in range(NT):
                pe.wait_ge(xn_done, t + 1)
                for k in range(KC - 1):
                    last = transpose(t, k)
                    if t == NT - 1:
                        last.then_inc(transposed, 1)
                if t == 1 and first_row:
                    for i in range(2):
                        pe.wait_ge(partial_loaded[i], 16)
                        last = sum_feature_major(nc, g, ps_T[:, i, :], partial[:, i, :])
                    last.then_inc(rows_summed, 1)
            if first_row:
                pe.wait_ge(modulation_ready, 1)
            for t in range(NT):
                last = transpose(t, KC - 1)
            last.then_inc(transposed, 1)

        @block.vector
        def _(dve):
            chain = Chain(dve, chain_s)
            nc.vector.tensor_scalar(mean_sq[:], g.sums[:], 1.0 / D, EPS, ALU.mult, ALU.add).then_inc(mean_done, 1)
            dve.wait_ge(std_done, 1)
            chain(nc.vector.reciprocal(rstd[:], std[:]))
            for t in range(NT):
                nc.vector.tensor_scalar(xn[t], g.x[:, t, :], rstd[:, t:t + 1], None, ALU.mult).then_inc(xn_done, 1)
            if first_row:
                dve.wait_ge(rows_summed, 1)
                dve.wait_ge(small_loaded, 32)
                feature_modulation(nc, g, chain, ps_T, bias_T, gain_T).then_inc(modulation_ready, 1)
                dve.wait_ge(modulation_ready, 1)
            for k in range(1, KC, 2):
                dve.wait_ge(transposed, k + 1)
                nc.vector.tensor_scalar(g.hT[:, k, :], ps_t[:, k, :], g.scale_T[:, k:k + 1], g.shift_T[:, k:k + 1],
                                        ALU.mult, ALU.add)


def attention_buffers(nc, g, scope):
    sb = lambda n, s, d=FP32: scope.enter_context(nc.sbuf_tensor(n, s, d))
    b = Shared()
    b.wq, b.wk, b.wv, b.wo = sb("wq", [P, KC, P]), sb("wk", [P, KC, P]), sb("wv", [P, KC, P]), sb("wo", [P, HEADS, D])
    b.q_loaded, b.k_loaded, b.v_loaded, b.wo_loaded = (g.sem(n) for n in ("q_loaded", "k_loaded", "v_loaded", "wo_loaded"))
    return b


def load_head(g, b, eng, h, part):
    w = g.inputs["da_w_in"][0, :, :].rearrange("(p k) (s h n) -> p k s h n", k=KC, s=3, n=P)
    dst, loaded = ((b.wq, b.q_loaded), (b.wk, b.k_loaded), (b.wv, b.v_loaded))[part]
    eng.dma_start(dst[:], w[:, :, part, ds(h, 1), :].rearrange("p k a n -> p k (a n)")).then_inc(loaded, 16)


def attention(nc, g, b):
    with ExitStack() as scope:
        sb = lambda n, s, d=FP32: scope.enter_context(nc.sbuf_tensor(n, s, d))
        qT, kT, v = sb("qT", [P, S]), sb("kT", [P, S]), sb("v", [P, NT, P])
        rot, rot2 = sb("rot", [P, S]), sb("rot2", [P, S])
        prob = sb("prob", [P, 8, S])
        neg_max, row_sum, inv_sum, lam_inv = (sb(n, [P, 8]) for n in ("neg_max", "row_sum", "inv_sum", "lam_inv"))
        aT = [sb(f"aT{i}", [P, NT, P]) for i in range(NT)]
        osq, on = sb("osq", [P, NT, P]), sb("on", [P, NT, P])
        o_sum, o_ms, o_std, o_inv = (sb(n, [P, NT]) for n in ("o_sum", "o_ms", "o_std", "o_inv"))
        oT = sb("oT", [P, HEADS, S])
        mix = sb("mix", [P, 2, BANK])
        gate_b = g.squares[0:1, :]
        ps_s = [scope.enter_context(nc.psum_tensor(f"ps_s{i}", [P, BANK], FP32)) for i in range(4)]
        ps_kv = scope.enter_context(nc.psum_tensor("ps_kv", [P, 2 * BANK], FP32))
        ps_k, ps_v = ps_kv[:, 0:BANK], ps_kv[:, BANK:]
        ps_q, ps_o = (scope.enter_context(nc.psum_tensor(n, [P, BANK], FP32)) for n in ("ps_q", "ps_o"))
        sem = g.stage_semaphores(scope, "")
        qk_projected, v_projected, v_copied, rotated = sem("qk_projected"), sem("v_projected"), sem("v_copied"), sem("rotated")
        scored, maxed, exped, mixed = sem("scored"), sem("maxed"), sem("exped"), sem("mixed")
        a_transposed, a_copied, weighted, o_squared = sem("a_transposed"), sem("a_copied"), sem("weighted"), sem("o_squared")
        o_mean, o_rooted, o_normed, o_transposed = sem("o_mean"), sem("o_rooted"), sem("o_normed"), sem("o_transposed")
        o_copied, chain_s, projected_out, added = sem("o_copied"), sem("att_chain"), sem("projected_out"), sem("att_added")
        ada_loaded, ada_used, ada_chain = [sem(f"ada_loaded{i}") for i in range(2)], sem("ada_used"), sem("ada_chain")
        partial_done, partial_free, partial_stored = sem("partial_done"), sem("partial_free"), g.sem("partial_stored0")
        gate_loaded, gate_summed, gate_done = sem("gate_loaded"), sem("gate_summed"), sem("gate_done")
        g.squared = sem("att_squared")
        block = scope.enter_context(nc.Block())
        FIRST_ADA, ADA_ROWS = 2, HEADS - 1
        HOPS = 10

        @block.gpsimd
        def _(pool):
            pool.sem_clear(g.other_semaphores)
            store_partials(g, pool, FIRST_ADA, ADA_ROWS, partial_done, partial_stored, partial_free)

        @block.sync
        def _(sp):
            sp.dma_start(gate_b[:], g.inputs["ada_b"][0:1, 2 * D:3 * D]).then_inc(gate_loaded, 16)
            sp.dma_start(b.wo[:], g.inputs["da_w_out"][0, :, :].rearrange("(h p) n -> p h n", p=P)).then_inc(b.wo_loaded, 16)
            with sp.Fori(1, HEADS) as h:
                sp.wait_ge(qk_projected, 2 * h - 1)
                load_head(g, b, sp, h, 0)
                sp.wait_ge(qk_projected, 2 * h)
                load_head(g, b, sp, h, 1)
                sp.wait_ge(v_projected, h)
                load_head(g, b, sp, h, 2)
                for half in range(2):
                    sp.wait_ge(ada_used, 2 * (h - 1) + half + 1)
                    load_ada(g, sp, FIRST_ADA + h - 1, half, ada_loaded[half])
            sp.wait_ge(ada_used, 2 * ADA_ROWS + 2)
            sp.wait_ge(partial_free, ADA_ROWS + 1)
            sp.dma_start(g.partial[:], g.mod_dram[2, :, :]).then_inc(gate_loaded, 16)
            g.load_expert(sp, 0, 0, 0)
            g.load_expert(sp, 0, 1, 1)

        @block.tensor
        def _(pe):
            def project_qk(h):
                for w, loaded, ps in ((b.wq, b.q_loaded, ps_q), (b.wk, b.k_loaded, ps_k)):
                    pe.wait_ge(loaded, 16 * h + 16)
                    for k in range(KC):
                        last = nc.tensor.matmul(ps[:], w[:, k, :], g.hT[:, k, :], start=(k == 0), stop=(k == KC - 1))
                    last.then_inc(qk_projected, 1)

            def project_v(h):
                pe.wait_ge(b.v_loaded, 16 * h + 16)
                after(pe, o_copied, h - 1)
                for t in range(NT):
                    for k in range(KC):
                        last = nc.tensor.matmul(ps_v[:, t * P:(t + 1) * P], g.hT[:, k, t * P:(t + 1) * P], b.wv[:, k, :],
                                                start=(k == 0), stop=(k == KC - 1))
                last.then_inc(v_projected, 1)

            def scores(h):
                pe.wait_ge(rotated, 2 * h + 2)
                for u in range(8):
                    t, c = divmod(u, 2)
                    if u < 4:
                        pe.wait_ge(a_copied, 4 * h + u + 1)
                    else:
                        pe.wait_ge(exped, 8 * h + u - 3)
                    rows = slice(HD * c, HD * c + HD)
                    nc.tensor.matmul(ps_s[u % 4][:], qT[rows, t * P:(t + 1) * P], kT[rows, :], start=True, stop=True)\
                        .then_inc(scored, 1)

            def transpose_probs(h, t):
                pe.wait_ge(mixed, 4 * h + t + 1)
                for c in range(NT):
                    last = nc.tensor.transpose(ps_s[t][:, c * P:(c + 1) * P], prob[:, 2 * t, c * P:(c + 1) * P], g.ident[:])
                last.then_inc(a_transposed, 1)

            def weigh_values(h, t):
                pe.wait_ge(a_copied, 4 + 4 * h + t + 1)
                if t == 0:
                    pe.wait_ge(v_copied, h + 1)
                    pe.wait_ge(o_normed, h + 1)
                for c in range(NT):
                    last = nc.tensor.matmul(ps_o[:, t * P:(t + 1) * P], aT[t][:, c, :], v[:, c, :],
                                            start=(c == 0), stop=(c == NT - 1))
                if t == NT - 1:
                    last.then_inc(weighted, 1)

            def values(h):
                transpose_probs(h, 0)
                for t in range(1, NT):
                    transpose_probs(h, t)
                    weigh_values(h, t - 1)
                weigh_values(h, NT - 1)

            def transpose_outputs(h, ps):
                pe.wait_ge(o_normed, h + 2)
                if ps is ps_v:
                    pe.wait_ge(v_copied, h + 2)
                for t in range(NT):
                    last = nc.tensor.transpose(ps[:, t * P:(t + 1) * P], on[:, t, :], g.ident[:])
                last.then_inc(o_transposed, 1)

            project_qk(0)
            project_v(0)
            scores(0)
            project_qk(1)
            values(0)
            project_v(1)
            with pe.Fori(1, HEADS - 1) as h:
                scores(h)
                transpose_outputs(h - 1, ps_v)
                project_qk(h + 1)
                values(h)
                project_v(h + 1)
            scores(HEADS - 1)
            transpose_outputs(HEADS - 2, ps_v)
            pe.wait_ge(gate_loaded, 32)
            pe.wait_ge(o_copied, HEADS - 1)
            sum_conditioning(nc, g, g.partial, gate_b, ps_kv).then_inc(gate_summed, 1)
            values(HEADS - 1)
            transpose_outputs(HEADS - 1, ps_q)
            pe.wait_ge(b.wo_loaded, 16)
            pe.wait_ge(o_copied, HEADS)
            pe.wait_ge(gate_done, 1)
            for i, ps in enumerate([*ps_s, ps_k, ps_v, ps_o, ps_q]):
                t, n = divmod(i, 2)
                for h in range(HEADS):
                    last = nc.tensor.matmul(ps[:], oT[:, h, t * P:(t + 1) * P], b.wo[:, h, n * BANK:(n + 1) * BANK],
                                            start=(h == 0), stop=(h == HEADS - 1))
                last.then_inc(projected_out, 1)

        @block.scalar
        def _(act):
            def copy_v(h):
                act.wait_ge(v_projected, h + 1)
                nc.scalar.activation(v[:].rearrange("p t n -> p (t n)"), ps_v, ACT.Copy).then_inc(v_copied, 1)

            def copy_outputs(h, ps):
                act.wait_ge(o_transposed, h + 1)
                nc.scalar.activation(oT[:, ds(h, 1), :].rearrange("p a n -> p (a n)"), ps, ACT.Copy,
                                     scale=g.subln[:]).then_inc(o_copied, 1)

            def head(h, previous_outputs):
                for u in range(8):
                    act.wait_ge(maxed, 8 * h + u + 1)
                    nc.scalar.activation(prob[:, u, :], ps_s[u % 4][:], ACT.Exp, bias=neg_max[:, u:u + 1],
                                         accum_out=row_sum[:, u:u + 1]).then_inc(exped, 1)
                if previous_outputs:
                    copy_outputs(h - 1, ps_v)
                for t in range(NT):
                    act.wait_ge(a_transposed, 4 * h + t + 1)
                    nc.scalar.activation(aT[t][:].rearrange("p c n -> p (c n)"), ps_s[t][:], ACT.Copy).then_inc(a_copied, 1)
                act.wait_ge(weighted, h + 1)
                nc.scalar.activation(osq[:].rearrange("p t n -> p (t n)"), ps_o[:], ACT.Square).then_inc(o_squared, 1)
                act.wait_ge(o_mean, h + 1)
                nc.scalar.activation(o_std[:], o_ms[:], ACT.Sqrt).then_inc(o_rooted, 1)

            act.sem_inc(a_copied, 4)
            copy_v(0)
            head(0, False)
            copy_v(1)
            with act.Fori(1, HEADS - 1) as h:
                head(h, True)
                copy_v(h + 1)
            head(HEADS - 1, True)
            act.wait_ge(gate_summed, 1)
            nc.scalar.activation(g.gate[:], ps_kv[:], ACT.Copy).then_inc(gate_done, 1)
            copy_outputs(HEADS - 1, ps_q[:])
            square_tiles(nc, g, act, added, 2)

        @block.vector
        def _(dve):
            def rotate(h, chain, between=None):
                for i, (ps, dst) in enumerate(((ps_q, qT), (ps_k, kT))):
                    factor = HD ** -0.5 if i == 0 else 1.0
                    dve.wait_ge(qk_projected, 2 * h + 1 + i)
                    for q in range(4):
                        rows, other = slice(32 * q, 32 * q + 32), slice(32 * (q ^ 1), 32 * (q ^ 1) + 32)
                        nc.vector.scalar_tensor_tensor(rot[rows, :], ps[other, :], factor, g.sin[other, :],
                                                       ALU.mult, ALU.mult)
                    chain(nc.vector.scalar_tensor_tensor(rot2[:], ps[:], factor, g.cos[:], ALU.mult, ALU.mult))
                    nc.vector.tensor_tensor(dst[:], rot[:], rot2[:], ALU.add).then_inc(rotated, 1)
                    if between and i == 0:
                        between()
                    dve.wait_ge(rotated, 2 * h + 1 + i)

            def ada(h, chunks):
                for k in chunks:
                    if k == 0:
                        dve.wait_ge(partial_free, h + 1)
                    if k % ADA_HALF == 0:
                        dve.wait_ge(ada_loaded[k // ADA_HALF], 16 * h + 16)
                    add_ada(nc, g, dve, [k], ada_chain, h, ada_used, partial_done)

            def head(h, last):
                chain = Chain(dve, chain_s, 2 + HOPS * h)
                for u in range(8):
                    dve.wait_ge(scored, 8 * h + u + 1)
                    nc.vector.tensor_reduce(neg_max[:, u:u + 1], ps_s[u % 4][:], AX.X, ALU.max, negate=True)\
                        .then_inc(maxed, 1)
                dve.wait_ge(exped, 8 * h + 8)
                chain(nc.vector.reciprocal(inv_sum[:], row_sum[:]))
                chain(nc.vector.tensor_scalar(lam_inv[:], inv_sum[:], g.neg_lam[:], None, ALU.mult))
                for t in range(NT):
                    nc.vector.tensor_scalar(prob[:, 2 * t + 1, :], prob[:, 2 * t + 1, :], lam_inv[:, 2 * t + 1:2 * t + 2],
                                            None, ALU.mult).then_inc(chain_s, 1)
                    chain.n += 1
                for t in range(NT):
                    dve.wait_ge(chain_s, chain.base + 3 + t)
                    nc.vector.scalar_tensor_tensor(prob[:, 2 * t, :], prob[:, 2 * t, :], inv_sum[:, 2 * t:2 * t + 1],
                                                   prob[:, 2 * t + 1, :], ALU.mult, ALU.add).then_inc(mixed, 1)
                if not last:
                    ada(h, range(1))
                    rotate(h + 1, chain, lambda: ada(h, range(1, 3)))
                    ada(h, range(3, 4))
                dve.wait_ge(o_squared, h + 1)
                chain(nc.vector.reduce_sum(o_sum[:], osq[:], AX.X))
                nc.vector.tensor_scalar(o_ms[:], o_sum[:], 1.0 / P, EPS, ALU.mult, ALU.add).then_inc(o_mean, 1)
                dve.wait_ge(o_rooted, h + 1)
                chain(nc.vector.reciprocal(o_inv[:], o_std[:]))
                nc.vector.tensor_tensor(on[:], ps_o[:].rearrange("p (t n) -> p t n", n=P),
                                        o_inv[:].unsqueeze(2).to_broadcast([P, NT, P]), ALU.mult).then_inc(o_normed, 1)
                if not last:
                    ada(h, range(4, KC))
                assert chain.n == (HOPS - 2 if last else HOPS)

            dve.sem_inc(o_normed, 1)
            dve.sem_inc(ada_used, 2)
            rotate(0, Chain(dve, chain_s))
            with dve.Fori(0, HEADS - 1) as h:
                head(h, False)
            head(HEADS - 1, True)
            add_gated(nc, g, dve, chain_s, 2 + HOPS * HEADS - 2, projected_out, added,
                      [*ps_s, ps_k, ps_v, ps_o, ps_q], mix, (gate_done, 1))


def add_gated(nc, g, dve, chain_s, base, ready, added, banks, scratch, gate_ready=None):
    if gate_ready:
        dve.wait_ge(*gate_ready)
    for i, ps in enumerate(banks):
        t, n = divmod(i, 2)
        cols = slice(n * BANK, (n + 1) * BANK)
        dve.wait_ge(ready, i + 1)
        if i >= 2:
            dve.wait_ge(added, i - 1)
        nc.vector.tensor_tensor(scratch[:, i % 2, :], ps[:], g.gate[:, cols], ALU.mult).then_inc(chain_s, 1)
        dve.wait_ge(chain_s, base + i + 1)
        nc.vector.tensor_tensor(g.x[:, t, cols], g.x[:, t, cols], scratch[:, i % 2, :], ALU.add).then_inc(added, 1)


def experts_buffers(nc, g, layer, scope):
    sb = lambda n: scope.enter_context(nc.sbuf_tensor(f"moe{layer}_{n}", [P, D], FP32))
    b = Shared()
    b.xg, b.out = [sb(f"xg{i}") for i in range(2)], [sb(f"out{i}") for i in range(2)]
    b.xn = [t[:] for t in (*b.xg, *b.out)]
    return b


def experts(nc, g, b, layer):
    A = g.inputs
    xg, out, xn = b.xg, b.out, b.xn
    tag = f"moe{layer}"
    with ExitStack() as scope:
        sb = lambda n, s, d=FP32: scope.enter_context(nc.sbuf_tensor(f"{tag}_{n}", s, d))
        ring_hi = sb("ring_hi", [P, 2, SLOT])
        slots = [g.ring[:, 0, :], g.ring[:, 1, :], ring_hi[:, 0, :], ring_hi[:, 1, :]]
        w_gate = [s[:, 0:KC * F].rearrange("p (k f) -> p k f", k=KC) for s in slots]
        w_up = [s[:, KC * F:2 * KC * F].rearrange("p (k f) -> p k f", k=KC) for s in slots]
        w_down = [s[:, 2 * KC * F:].rearrange("p (j n) -> p j n", j=2) for s in slots]
        SHARED = RING - 3
        w_router = sb("w_router", [P, KC, E])
        bias = sb("bias", [P, E])
        tile3 = [P, NT, E]
        score, select = sb("score", tile3), sb("select", tile3)
        top8 = sb("top8", [P, NT, EXPERT_GROUPS, 8])
        group_score = sb("group_score", [P, NT, EXPERT_GROUPS])
        above, equal = sb("above", [P, NT, 8, 8]), sb("equal", [P, NT, 8, 8])
        group_in, group_out = sb("group_in", [P, NT, 8]), sb("group_out", [P, NT, 8])
        top_sel = sb("top_sel", [P, NT, 8])
        greater, tied, chosen = sb("greater", tile3), sb("tied", tile3), sb("chosen", tile3)
        missing, weight_sum = sb("missing", [P, NT]), sb("weight_sum", [P, NT])
        place = sb("place", tile3)
        record = sb("record", [P, NT, E, 3])
        count_i = sb("count_i", [P, E + 1], I32)
        extra, done_before = sb("extra", [P, E]), sb("done_before", [P, E])
        over_f = sb("over_f", [P, 2])
        over_i = sb("over_i", [P, 2], I32)
        onehot = [sb(f"onehot{i}", [P, NT, P]) for i in range(2)]
        index = [sb(f"index{i}", [P, 2], I32) for i in range(RING)]
        weight = [sb(f"weight{i}", [P, 1]) for i in range(RING)]
        xT = [sb(f"xT{i}", [P, KC, P]) for i in range(2)]
        weight_hi = [sb(f"weight_hi{i}", [P, 1]) for i in range(RING)]
        silu = sb("silu", [P, 2, P])
        hid_tok = sb("hid_tok", [P, F])
        hid = [sb(f"hid{i}", [P, 2, P]) for i in range(2)]
        silu_all, hid_all = sb("silu_all", [P, 2, S]), sb("hid_all", [P, 2, S])
        total = [sb("total", [P, D])[:], g.partial[:]]
        partial = [ring_hi[:, 0, i * D:(i + 1) * D] for i in range(3)]
        ada_b = [ring_hi[0:1, 0, (3 + i) * D:(4 + i) * D] for i in range(3)]
        scale_row = xT[0][:].rearrange("p a b -> p (a b)")
        gain = total[1]

        ps = lambda n, s: scope.enter_context(nc.psum_tensor(f"{tag}_{n}", s, FP32))
        ps_r, ps_p = ps("ps_r", [P, 8, E]), ps("ps_p", [P, 8, E])
        pairs = [ps(n, [P, D]) for n in ("ps_ih", "ps_x", "ps_y")]
        halves = lambda pair: [pair[:, i * BANK:(i + 1) * BANK] for i in range(2)]
        four = lambda bank: bank.rearrange("p (a b) -> p a b", b=P)
        ps_i, ps_h = pairs[0][:, 0:BANK], four(pairs[0][:, BANK:])
        ps_x, ps_y = [four(half) for half in halves(pairs[1])], halves(pairs[2])
        ps_h_flat, silu_flat = pairs[0][:, BANK:], silu[:].rearrange("p a b -> p (a b)")
        ps_turned = ps_h_flat[:, F:].rearrange("p (j n) -> p j n", j=2)
        LOW, HIGH = slice(0, NARROW), slice(P - NARROW, P)
        shared_banks = [ps_r[:].rearrange("p a b -> p (a b)"), ps_p[:].rearrange("p a b -> p (a b)"), *halves(pairs[1])]

        sem = g.stage_semaphores(scope, f"{tag}_")
        router_loaded, routed, scored = sem("router_loaded"), sem("routed"), sem("scored")
        chain_s, chosen_done, placed = sem("chain"), sem("chosen_done"), sem("placed")
        over_done, over_stored = sem("over_done"), g.sem(f"over_stored{layer}")
        partial_loaded, bias_loaded, gain_loaded = [sem(f"partial_loaded{i}") for i in range(3)], sem("bias_loaded"), sem("gain_loaded")
        row_biased, row_summed, gate_copied = sem("row_biased"), sem("row_summed"), sem("gate_copied")
        h_done, h_stored = sem("h_done"), g.sem(f"h_stored{layer}")
        g.squared, x_updated, paired = sem("squared"), sem("x_updated"), sem("paired")
        pool_turns = sem("pool_turns")
        shared_up, shared_silu, shared_hid = sem("shared_up"), sem("shared_silu"), sem("shared_hid")
        shared_down, shared_added = sem("shared_down"), sem("shared_added")
        loaded = g.expert_loaded[layer]
        onehot_done, looked_up, index_done = sem("onehot_done"), sem("looked_up"), sem("index_done")
        gathered = [g.sem(f"gathered{layer}_{i}") for i in range(2)]
        x_transposed, x_copied, up_done, silu_done = sem("x_transposed"), sem("x_copied"), sem("up_done"), sem("silu_done")
        hid_rows, hid_turned = sem("hid_rows"), sem("hid_turned")
        hid_done, down_done, out_lo, out_hi = sem("hid_done"), sem("down_done"), sem("out_lo"), sem("out_hi")
        scattered = [g.sem(f"scattered{layer}_{i}") for i in range(2)]
        over_scattered, over_free, all_scattered = g.sem(f"over_scattered{layer}"), sem("over_free"), sem("all_scattered")
        rows_loaded, row_chain, totalled = [sem(f"rows_loaded{i}") for i in range(2)], sem("row_chain"), sem("totalled")
        block = scope.enter_context(nc.Block())

        def passes(eng, step):
            for s in range(RING):
                step(0, s, False)
            with eng.Fori(1, E // RING - 1) as r:
                for s in range(RING):
                    step(r, s, False)
            for s in range(RING):
                step(E // RING - 1, s, True)

        def by_width(eng, n, wide_step, narrow_step):
            tokens = eng.value_load(count_i[0:1, ds(n, 1)], min_val=0, max_val=S)
            with eng.If(tokens > NARROW):
                wide_step()
            with eng.Else():
                narrow_step()

        def extra_passes(eng, step):
            eng.wait_ge(over_stored, 32)
            n_extra = eng.value_load(g.over_dram[P:P + 1, 0:1], min_val=0, max_val=MAX_OVERFLOW)
            with eng.If(n_extra > 0):
                with eng.Fori(0, MAX_OVERFLOW // OVERFLOW_GROUP) as q:
                    with eng.If(OVERFLOW_GROUP * q < n_extra):
                        with eng.Fori(0, OVERFLOW_GROUP) as j:
                            with eng.If(OVERFLOW_GROUP * q + j < n_extra):
                                step(OVERFLOW_GROUP * q + j)
                            eng.nop()
                    eng.nop()

        def extra_expert(eng, i):
            return eng.value_load(g.over_dram[ds(i, 1), 0:1], min_val=0, max_val=E - 1)

        @block.sync
        def _(sp):
            for i, row in enumerate((4, 3, 5)):
                sp.dma_start(ada_b[i], A["ada_b"][layer:layer + 1, row * D:(row + 1) * D]).then_inc(bias_loaded, 16)

            def load_row(i, row):
                sp.dma_start(partial[i], g.mod_dram[6 * layer + row, :, :]).then_inc(partial_loaded[i], 16)

            load_row(0, 4)
            load_row(1, 3)
            sp.dma_start(gain, A["norm2_g"][layer, :].partition_broadcast(P)).then_inc(gain_loaded, 16)
            sp.dma_start(w_router[:], A["moe_w_router"][layer, :, :].rearrange("(p k) n -> p k n", k=KC)).then_inc(router_loaded, 16)
            sp.dma_start(bias[:], A["moe_router_bias"][layer, :].partition_broadcast(P)).then_inc(router_loaded, 16)
            load_row(2, 5)

            def step(r, s, tail):
                n = RING * r + s
                if isinstance(r, int) and r == 0:
                    if s < 2:
                        return
                    if s == 2:
                        sp.wait_ge(row_summed, 3)
                else:
                    sp.wait_ge(down_done, n - (RING - 1))
                g.load_expert_into(sp, layer, slots[s], s, n)

            def extra_step(i):
                e = extra_expert(sp, i)
                sp.wait_ge(down_done, E + i)
                g.load_expert_into(sp, layer, slots[0], 0, e)

            passes(sp, step)
            sp.wait_ge(down_done, E - 2)
            for dst, name in ((w_gate[SHARED], "moe_ws_gate"), (w_up[SHARED], "moe_ws_up")):
                sp.dma_start(dst, A[name][layer, :, :].rearrange("(p k) f -> p k f", k=KC)).then_inc(loaded[SHARED], 16)
            sp.dma_start(w_down[SHARED], A["moe_ws_down"][layer, :, :].rearrange("(j p) n -> p j n", p=P))\
                .then_inc(loaded[SHARED], 16)
            extra_passes(sp, extra_step)
            sp.wait_ge(all_scattered, 1)
            for t in range(NT):
                if t >= 2:
                    sp.wait_ge(totalled, t - 1)
                sp.dma_start(slots[2 + t % 2], g.rows_dram[t * P * TOP_K:(t + 1) * P * TOP_K, :]
                             .rearrange("(p k) d -> p (k d)", k=TOP_K)).then_inc(rows_loaded[t % 2], 16)
            for i in range(2):
                sp.wait_ge(rows_loaded[i], 32)

        @block.gpsimd
        def _(pool):
            pool.sem_clear(g.other_semaphores)
            for t in range(NT):
                pool.wait_ge(h_done, t + 1)
                pool.dma_start(g.h_dram[t * P:(t + 1) * P, :], xn[t]).then_inc(h_stored, 16)

            def move_filled(expert, move):
                tokens = pool.value_load(count_i[0:1, ds(expert, 1)], min_val=0, max_val=S)

                def between(low, high):
                    if high - low == ROW_STEP:
                        return move(high)
                    middle = (low + high) // 2
                    with pool.If(tokens > middle):
                        between(middle, high)
                    with pool.Else():
                        between(low, middle)

                between(0, P)

            def gather(n, s, expert):
                def move(rows):
                    pool.indirect_dma_start(out=xg[s % 2][0:rows, :], out_offset=None, in_=g.h_dram[:, :],
                                            in_offset=bass.IndirectOffsetOnAxis(ap=index[s][0:rows, 0:1], axis=0),
                                            bounds_check=S - 1, oob_is_err=False).then_inc(gathered[s % 2], 16)

                pool.wait_ge(index_done, n + 1)
                after(pool, x_transposed, n - 1)
                pool.sem_inc(pool_turns, 1)
                move_filled(expert, move)

            def scatter(n, s, expert, done):
                def move(rows):
                    pool.indirect_dma_start(out=g.rows_dram[:, :],
                                            out_offset=bass.IndirectOffsetOnAxis(ap=index[s][0:rows, 1:2], axis=0),
                                            in_=out[s % 2][0:rows, :], in_offset=None,
                                            bounds_check=S * TOP_K - 1, oob_is_err=False).then_inc(done, 16)

                pool.wait_ge(out_lo, n + 1)
                pool.wait_ge(out_hi, n + 1)
                pool.sem_inc(pool_turns, 1)
                move_filled(expert, move)

            def step(r, s, tail):
                n = RING * r + s
                if not tail or s < RING - 2:
                    gather(n + 2, (s + 2) % RING, n + 2)
                scatter(n, s, n, scattered[s % 2])

            def extra_step(i):
                e = extra_expert(pool, i)
                gather(E + i, 0, e)
                scatter(E + i, 0, e, over_scattered)
                pool.wait_ge(over_scattered, 16 * i + 16)
                pool.sem_inc(over_free, 1)

            pool.wait_ge(h_stored, 16 * NT)
            gather(0, 0, 0)
            gather(1, 1, 1)
            pool.wait_ge(over_done, 1)
            pool.dma_start(g.over_dram[0:P, :], over_i[:]).then_inc(over_stored, 16)
            pool.dma_start(g.over_dram[P:P + 1, 0:1], count_i[0:1, E:E + 1]).then_inc(over_stored, 16)
            passes(pool, step)
            for i in range(2):
                pool.wait_ge(scattered[i], 16 * E // 2)
            pool.sem_inc(over_free, 1)
            extra_passes(pool, extra_step)
            pool.sem_inc(all_scattered, 1)
            for t in range(NT):
                pool.wait_ge(rows_loaded[t % 2], 16 * (t // 2 + 1))
                rows = slots[2 + t % 2].rearrange("p (k d) -> p k d", d=D)
                nc.gpsimd.tensor_tensor(rows[:, TOP_K - 2, :], rows[:, TOP_K - 2, :], rows[:, TOP_K - 1, :], ALU.add)\
                    .then_inc(paired, 1)

        @block.tensor
        def _(pe):
            def sum_row(i):
                pe.wait_ge(row_biased, i + 1)
                sum_conditioning(nc, g, partial[i], None, pairs[(1, 2, 0)[i]]).then_inc(row_summed, 1)

            sum_row(0)
            sum_row(1)
            pe.wait_ge(router_loaded, 32)
            for t in range(NT):
                for k in range(KC):
                    last = nc.tensor.matmul(ps_r[:, t, :], g.hT[:, k, t * P:(t + 1) * P], w_router[:, k, :],
                                            start=(k == 0), stop=(k == KC - 1))
            last.then_inc(routed, 1)
            sum_row(2)
            pe.wait_ge(chosen_done, 1)
            for t in range(NT + 1):
                for u in range(min(t + 1, NT)):
                    last = nc.tensor.matmul(ps_p[:, t, :], (g.tri if u == t else g.ones)[:], chosen[:, u, :],
                                            start=(u == 0), stop=(u == min(t, NT - 1)))
            last.then_inc(placed, 1)

            def shared_expert():
                pe.wait_ge(loaded[SHARED], 48 * (E // RING + 1))
                for i in range(4):
                    w, j = (w_gate, w_up)[i // 2][SHARED], i % 2
                    for k in range(KC):
                        last = nc.tensor.matmul(shared_banks[i], w[:, k, j * P:(j + 1) * P], g.hT[:, k, :],
                                                start=(k == 0), stop=(k == KC - 1))
                    last.then_inc(shared_up, 1)
                for i in range(8):
                    t, n = divmod(i, 2)
                    if i == 0:
                        pe.wait_ge(shared_hid, 2)
                    if i >= 4:
                        pe.wait_ge(shared_added, i - 3)
                    for j in range(2):
                        last = nc.tensor.matmul(shared_banks[i % 4], hid_all[:, j, t * P:(t + 1) * P],
                                                w_down[SHARED][:, j, n * BANK:(n + 1) * BANK], start=(j == 0), stop=(j == 1))
                    last.then_inc(shared_down, 1)

            def look_up(n, s, expert):
                pe.wait_ge(onehot_done, n + 1)
                after(pe, index_done, n)
                for t in range(NT):
                    last = nc.tensor.matmul(ps_i[:, 0:3], onehot[s % 2][:, t, :],
                                            record[:, t, ds(expert, 1), :].rearrange("p a c -> p (a c)"),
                                            start=(t == 0), stop=(t == NT - 1))
                last.then_inc(looked_up, 1)

            def transpose_x(n, s, gathers):
                pe.wait_ge(gathered[s % 2], 16 * gathers)
                after(pe, x_copied, 2 * n)
                for k in range(KC):
                    last = nc.tensor.transpose(ps_x[k // 4][:, k % 4, :], xg[s % 2][:, k::KC], g.ident[:])
                last.then_inc(x_transposed, 1)

            def gate_up_ready(n, s, loads):
                pe.wait_ge(x_copied, 2 * n + 2)
                pe.wait_ge(loaded[s], 48 * loads)
                after(pe, hid_done, n)

            def gate_up(n, s):
                for i in range(4):
                    w, j = (w_gate, w_up)[i // 2][s], i % 2
                    for k in range(KC):
                        last = nc.tensor.matmul(ps_h[:, i, :], w[:, k, j * P:(j + 1) * P], xT[s % 2][:, k, :],
                                                start=(k == 0), stop=(k == KC - 1))
                last.then_inc(up_done, 1)

            def gate_up_narrow(n, s):
                for k in range(KC):
                    for w, rows in ((w_gate[s], LOW), (w_up[s], HIGH)):
                        last = nc.tensor.matmul(ps_h_flat[rows, 0:F], xT[s % 2][:, k, LOW], w[:, k, :],
                                                start=(k == 0), stop=(k == KC - 1))
                last.then_inc(up_done, 1)

            def turn_hidden(n):
                pe.wait_ge(hid_rows, n + 1)
                for j in range(2):
                    last = nc.tensor.transpose(ps_turned[:, j, :], hid_tok[:, j * P:(j + 1) * P], g.ident[:])
                last.then_inc(hid_turned, 1)

            def down_ready(n):
                pe.wait_ge(hid_done, n + 1)
                after(pe, out_lo, n)
                after(pe, out_hi, n)

            def down(n, s):
                down_ready(n)
                for i in range(2):
                    for j in range(2):
                        last = nc.tensor.matmul(ps_y[i][:], hid[s % 2][:, j, :], w_down[s][:, j, i * BANK:(i + 1) * BANK],
                                                start=(j == 0), stop=(j == 1))
                last.then_inc(down_done, 1)

            def down_narrow(n, s):
                down_ready(n)
                for j in range(2):
                    for i, rows in enumerate((LOW, HIGH)):
                        last = nc.tensor.matmul(ps_y[0][rows, :], hid[s % 2][:, j, LOW],
                                                w_down[s][:, j, i * BANK:(i + 1) * BANK], start=(j == 0), stop=(j == 1))
                last.then_inc(down_done, 1)

            def step(r, s, tail):
                n = RING * r + s

                def look_ahead():
                    if not tail or s < RING - 2:
                        look_up(n + 2, (s + 2) % RING, n + 2)

                def transpose_next():
                    if not tail or s < RING - 1:
                        transpose_x(n + 1, (s + 1) % RING, 2 * r + (s + 1) // 2 + 1)

                def wide_step():
                    gate_up(n, s)
                    look_ahead()
                    transpose_next()
                    down(n, s)
                    pe.sem_inc(hid_turned, 1)

                def narrow_step():
                    gate_up_narrow(n, s)
                    look_ahead()
                    turn_hidden(n)
                    transpose_next()
                    down_narrow(n, s)

                gate_up_ready(n, s, r + 1)
                by_width(pe, n, wide_step, narrow_step)

            def extra_step(i):
                e = extra_expert(pe, i)
                look_up(E + i, 0, e)
                transpose_x(E + i, 0, E // 2 + 1 + i)
                gate_up_ready(E + i, 0, E // RING + 1 + i)
                gate_up(E + i, 0)
                down(E + i, 0)

            pe.wait_ge(gate_copied, 1)
            look_up(0, 0, 0)
            look_up(1, 1, 1)
            transpose_x(0, 0, 1)
            passes(pe, step)
            extra_passes(pe, extra_step)
            shared_expert()

        @block.scalar
        def _(act):
            act.wait_ge(routed, 1)
            nc.scalar.activation(score[:], ps_r[:, 0:NT, :], ACT.Sigmoid).then_inc(scored, 1)
            act.wait_ge(row_summed, 3)
            nc.scalar.activation(g.gate[:], pairs[0][:], ACT.Copy).then_inc(gate_copied, 1)

            def copy_x(n, s):
                act.wait_ge(x_transposed, n + 1)
                after(act, up_done, n - 1)
                for half in range(2):
                    nc.scalar.activation(xT[s % 2][:, 4 * half:4 * half + 4, :], ps_x[half][:], ACT.Copy).then_inc(x_copied, 1)

            def silu_ready(n):
                act.wait_ge(up_done, n + 1)
                after(act, hid_done, n)

            def out_ready(n, s, scatters):
                act.wait_ge(down_done, n + 1)
                if scatters is not None:
                    after(act, scattered[s % 2], scatters)

            def silu_gate(n):
                silu_ready(n)
                nc.scalar.activation(silu[:], ps_h[:, 0:2, :], ACT.Silu).then_inc(silu_done, 1)

            def scale_out(n, s, scatters):
                out_ready(n, s, scatters)
                nc.scalar.activation(out[s % 2][:, 0:BANK], ps_y[0][:], ACT.Copy, scale=weight[s][:]).then_inc(out_lo, 1)

            def step(r, s, tail):
                n = RING * r + s

                def copy_next():
                    if not tail or s < RING - 1:
                        copy_x(n + 1, (s + 1) % RING)

                def wide_step():
                    silu_gate(n)
                    copy_next()
                    scale_out(n, s, 16 * (2 * r + s // 2))

                def narrow_step():
                    silu_ready(n)
                    nc.scalar.activation(silu_flat[HIGH, 0:F], ps_h_flat[LOW, 0:F], ACT.Silu).then_inc(silu_done, 1)
                    copy_next()
                    out_ready(n, s, 16 * (2 * r + s // 2))
                    nc.scalar.activation(out[s % 2][LOW, 0:BANK], ps_y[0][LOW, :], ACT.Copy, scale=weight[s][LOW, :])\
                        .then_inc(out_lo, 1)

                by_width(act, n, wide_step, narrow_step)

            def extra_step(i):
                copy_x(E + i, 0)
                silu_gate(E + i)
                scale_out(E + i, 0, None)

            copy_x(0, 0)
            passes(act, step)
            extra_passes(act, extra_step)
            for j in range(2):
                act.wait_ge(shared_up, j + 1)
                nc.scalar.activation(silu_all[:, j, :], shared_banks[j], ACT.Silu).then_inc(shared_silu, 1)
            square_tiles(nc, g, act, x_updated, 1)

        @block.vector
        def _(dve):
            chain = Chain(dve, chain_s)
            tt, ts = nc.vector.tensor_tensor, nc.vector.tensor_scalar
            chain(nc.vector.memset(hid_tok[:], 0.0))
            dve.wait_ge(bias_loaded, 48)

            def add_bias(i):
                dve.wait_ge(partial_loaded[i], 16)
                tt(partial[i][0:1, :], partial[i][0:1, :], ada_b[i], ALU.add).then_inc(row_biased, 1)

            add_bias(0)
            add_bias(1)
            dve.wait_ge(gain_loaded, 16)
            dve.wait_ge(row_summed, 1)
            chain(nc.vector.scalar_tensor_tensor(scale_row, pairs[1][:], 1.0, gain, ALU.add, ALU.mult))
            for t in range(NT):
                chain(tt(xn[t], xn[t], scale_row, ALU.mult))
                if t == 0:
                    dve.wait_ge(row_summed, 2)
                tt(xn[t], xn[t], pairs[2][:], ALU.add).then_inc(h_done, 1)
            add_bias(2)
            dve.wait_ge(router_loaded, 32)
            dve.wait_ge(scored, 1)
            chain(tt(select[:], score[:], bias[:].unsqueeze(1).to_broadcast(tile3), ALU.add))
            for t in range(NT):
                for x in range(EXPERT_GROUPS):
                    last = nc.vector.max(top8[:, t, x, :], select[:, t, 8 * x:8 * x + 8])
            chain(last)
            chain(tt(group_score[:], top8[:, :, :, 0], top8[:, :, :, 1], ALU.add))
            pair = [P, NT, 8, 8]
            that, this = group_score[:].unsqueeze(2).to_broadcast(pair), group_score[:].unsqueeze(3).to_broadcast(pair)
            tt(above[:], that, this, ALU.is_gt)
            chain(tt(equal[:], that, this, ALU.is_equal))
            chain(tt(equal[:], equal[:], g.group_lower[:].unsqueeze(1).to_broadcast(pair), ALU.mult))
            chain(tt(above[:], above[:], equal[:], ALU.add))
            chain(nc.vector.reduce_sum(group_in[:], above[:], AX.X))
            chain(ts(group_in[:], group_in[:], float(TOPK_GROUPS), None, ALU.is_lt))
            chain(ts(group_out[:], group_in[:], 1e30, -1e30, ALU.mult, ALU.add))
            wide = lambda a: a[:].unsqueeze(3).to_broadcast(pair)
            split = lambda a: a[:].rearrange("p t (x e) -> p t x e", e=8)
            chain(tt(split(select), split(select), wide(group_in), ALU.mult))
            chain(tt(split(select), split(select), wide(group_out), ALU.add))
            for t in range(NT):
                last = nc.vector.max(top_sel[:, t, :], select[:, t, :])
            chain(last)
            sixth = top_sel[:, :, TOP_K - 1:TOP_K].to_broadcast(tile3)
            tt(greater[:], select[:], sixth, ALU.is_gt)
            chain(tt(g.prefix[:, 0, :, PAD:], select[:], sixth, ALU.is_equal))
            chain(nc.vector.reduce_sum(missing[:], greater[:], AX.X))
            chain(ts(missing[:], missing[:], -1.0, float(TOP_K), ALU.mult, ALU.add))

            def running_sum():
                for i in range(6):
                    a, b, shift = i % 2, (i + 1) % 2, 1 << i
                    chain(tt(g.prefix[:, b, :, PAD:], g.prefix[:, a, :, PAD:],
                             g.prefix[:, a, :, PAD - shift:PAD + E - shift], ALU.add))

            chain(nc.vector.tensor_copy(tied[:], g.prefix[:, 0, :, PAD:]))
            running_sum()
            chain(tt(g.prefix[:, 0, :, PAD:], g.prefix[:, 0, :, PAD:], tied[:], ALU.subtract))
            chain(tt(g.prefix[:, 0, :, PAD:], g.prefix[:, 0, :, PAD:], missing[:].unsqueeze(2).to_broadcast(tile3), ALU.is_lt))
            chain(tt(tied[:], tied[:], g.prefix[:, 0, :, PAD:], ALU.mult))
            tt(chosen[:], greater[:], tied[:], ALU.add).then_inc(chosen_done, 1)
            dve.wait_ge(chosen_done, 1)
            chain(tt(score[:], score[:], chosen[:], ALU.mult))
            chain(nc.vector.reduce_sum(weight_sum[:], score[:], AX.X))
            chain(nc.vector.reciprocal(weight_sum[:], weight_sum[:]))
            chain(tt(score[:], score[:], weight_sum[:].unsqueeze(2).to_broadcast(tile3), ALU.mult))
            ts(record[:, :, :, 2], score[:], ROUTED_SCALE, None, ALU.mult)
            chain(nc.vector.tensor_copy(g.prefix[:, 0, :, PAD:], chosen[:]))
            running_sum()
            chain(tt(g.prefix[:, 0, :, PAD:], g.prefix[:, 0, :, PAD:], chosen[:], ALU.subtract))
            tt(record[:, :, :, 1], g.prefix[:, 0, :, PAD:], g.row_shift[:].unsqueeze(2).to_broadcast(tile3), ALU.add)
            nc.vector.tensor_copy(record[:, :, :, 0], g.tok_shift[:].unsqueeze(2).to_broadcast(tile3))
            dve.wait_ge(placed, 1)
            chain(nc.vector.scalar_tensor_tensor(place[:], ps_p[:, 0:NT, :], 1.0, chosen[:], ALU.add, ALU.mult))
            chain(ts(place[:], place[:], -1.0, None, ALU.add))
            counts = ps_p[:, NT, :]
            nc.vector.tensor_copy(count_i[:, 0:E], counts)

            def one_hot(n, s, expert, places):
                after(dve, looked_up, n - 1)
                tt(onehot[s % 2][:], g.iota[:, places].unsqueeze(1).to_broadcast([P, NT, P]),
                   place[:, :, ds(expert, 1)].to_broadcast([P, NT, P]), ALU.is_equal).then_inc(onehot_done, 1)

            def indices(n, s, scatters):
                dve.wait_ge(looked_up, n + 1)
                if scatters is not None:
                    after(dve, scattered[s % 2], scatters)
                nc.vector.tensor_copy(weight[s][:], ps_i[:, 2:3])
                nc.vector.tensor_copy(weight_hi[s][HIGH, :], ps_i[LOW, 2:3])
                ts(index[s][:], ps_i[:, 0:2], SKIP, None, ALU.add).then_inc(index_done, 1)

            def hidden(n, s):
                dve.wait_ge(silu_done, n + 1)
                after(dve, down_done, n - 1)
                tt(hid[s % 2][:], silu[:], ps_h[:, 2:4, :], ALU.mult).then_inc(hid_done, 1)

            def out_ready(n, s, scatters):
                dve.wait_ge(down_done, n + 1)
                if scatters is not None:
                    after(dve, scattered[s % 2], scatters)

            def scale_out(n, s, scatters):
                out_ready(n, s, scatters)
                ts(out[s % 2][:, BANK:], ps_y[1][:], weight[s][:], None, ALU.mult).then_inc(out_hi, 1)

            def step(r, s, tail):
                n = RING * r + s

                def indices_ahead():
                    if not tail or s < RING - 2:
                        indices(n + 2, (s + 2) % RING, 16 * (2 * r + s // 2))

                def wide_step():
                    hidden(n, s)
                    dve.sem_inc(hid_rows, 1)
                    indices_ahead()
                    scale_out(n, s, 16 * (2 * r + s // 2))

                def narrow_step():
                    dve.wait_ge(silu_done, n + 1)
                    tt(hid_tok[LOW, :], silu_flat[HIGH, 0:F], ps_h_flat[HIGH, 0:F], ALU.mult).then_inc(hid_rows, 1)
                    indices_ahead()
                    dve.wait_ge(hid_turned, n + 1)
                    after(dve, down_done, n - 1)
                    nc.vector.tensor_copy(hid[s % 2][:, :, LOW], ps_turned[:, :, LOW]).then_inc(hid_done, 1)
                    out_ready(n, s, 16 * (2 * r + s // 2))
                    ts(out[s % 2][LOW, BANK:], ps_y[0][HIGH, :], weight_hi[s][HIGH, :], None, ALU.mult).then_inc(out_hi, 1)

                if not tail or s < RING - 3:
                    one_hot(n + 3, (s + 3) % RING, n + 3, slice(0, P))
                by_width(dve, n, wide_step, narrow_step)

            def extra_step(i):
                e = extra_expert(dve, i)
                block_of = dve.value_load(g.over_dram[ds(i, 1), 1:2], min_val=0, max_val=S // P - 1)
                one_hot(E + i, 0, e, ds(block_of * P, P))
                dve.wait_ge(over_free, i + 1)
                indices(E + i, 0, None)
                hidden(E + i, 0)
                scale_out(E + i, 0, None)

            one_hot(0, 0, 0, slice(0, P))
            one_hot(1, 1, 1, slice(0, P))
            indices(0, 0, 0)
            indices(1, 1, 0)
            one_hot(2, 2, 2, slice(0, P))
            chain(ts(extra[:], counts, float(SLOTS_PER_BLOCK), None, ALU.is_gt))
            for c in range(2, S // SLOTS_PER_BLOCK):
                chain(nc.vector.scalar_tensor_tensor(extra[:], counts, float(c * SLOTS_PER_BLOCK), extra[:], ALU.is_gt, ALU.add))
            chain(nc.vector.tensor_copy(g.prefix[:, 0, 0, PAD:], extra[:]))
            running_sum()
            ts(count_i[:, E:E + 1], g.prefix[:, 0, 0, PAD + E - 1:PAD + E], 0.0, None, ALU.add)
            chain(ts(done_before[:], g.prefix[:, 0, 0, PAD:], g.tok[:, 0:1], None, ALU.is_le))
            chain(nc.vector.reduce_sum(over_f[:, 0:1], done_before[:], AX.X))
            chain(tt(done_before[:], done_before[:], extra[:], ALU.mult))
            chain(nc.vector.reduce_sum(over_f[:, 1:2], done_before[:], AX.X))
            ts(over_i[:, 0:1], over_f[:, 0:1], float(E - 1), None, ALU.min)
            chain(tt(over_f[:, 1:2], g.tok[:, 0:1], over_f[:, 1:2], ALU.subtract))
            ts(over_i[:, 1:2], over_f[:, 1:2], 1.0, None, ALU.add).then_inc(over_done, 1)
            passes(dve, step)
            extra_passes(dve, extra_step)

            def sum_rows(t):
                dve.wait_ge(rows_loaded[t % 2], 16 * (t // 2 + 1))
                rows = slots[2 + t % 2].rearrange("p (k d) -> p k d", d=D)
                chain(tt(total[t % 2], rows[:, 0, :], rows[:, 1, :], ALU.add))
                for k in range(2, TOP_K - 2):
                    chain(tt(total[t % 2], total[t % 2], rows[:, k, :], ALU.add))
                dve.wait_ge(paired, t + 1)
                tt(total[t % 2], total[t % 2], rows[:, TOP_K - 2, :], ALU.add).then_inc(totalled, 1)
                dve.wait_ge(totalled, t + 1)

            def finish(t):
                for n in range(2):
                    half = total[t % 2][:, n * BANK:(n + 1) * BANK]
                    dve.wait_ge(shared_down, 2 * t + n + 1)
                    tt(half, half, shared_banks[(2 * t + n) % 4], ALU.add).then_inc(shared_added, 1)
                dve.wait_ge(shared_added, 2 * t + 2)
                chain(tt(total[t % 2], total[t % 2], g.gate[:], ALU.mult))
                tt(g.x[:, t, :], g.x[:, t, :], total[t % 2], ALU.add).then_inc(x_updated, 1)

            dve.wait_ge(gate_copied, 1)
            sum_rows(0)
            for j in range(2):
                dve.wait_ge(shared_silu, j + 1)
                dve.wait_ge(shared_up, j + 3)
                tt(hid_all[:, j, :], silu_all[:, j, :], shared_banks[2 + j], ALU.mult).then_inc(shared_hid, 1)
            sum_rows(1)
            for t in range(2, NT):
                finish(t - 2)
                dve.wait_ge(x_updated, t - 1)
                sum_rows(t)
            finish(NT - 2)
            finish(NT - 1)


N_IN = 2 * SG_HALF // BANK
K_OUT = SG_HALF // P


def gating_buffers(nc, g, scope):
    ring = scope.enter_context(nc.sbuf_tensor("w_in_ring", [P, 2 * KC, BANK], FP32))
    b = Shared()
    b.ring, b.w_in = ring, [ring[:, i * KC:(i + 1) * KC, :] for i in range(2)]
    b.loaded = [g.sem(f"w_in_loaded{i}") for i in range(2)]
    return b


def load_w_in(g, b, eng, n, i):
    rows = g.inputs["sg_w_in"][0, :, :].rearrange("(p k) n -> p k n", k=KC)
    eng.dma_start(b.w_in[i], rows[:, :, ds(n * BANK, BANK)]).then_inc(b.loaded[i], 16)


def gating(nc, g, b):
    A = g.inputs
    with ExitStack() as scope:
        sb = lambda n, s, d=FP32: scope.enter_context(nc.sbuf_tensor(f"sg_{n}", s, d))
        z = sb("z", [P, NT, 2 * SG_HALF])
        usT = b.ring
        hT_flat = g.hT[:].rearrange("p k t -> p (k t)")
        ln_g, ln_b = hT_flat[:, 0:SG_HALF], hT_flat[:, SG_HALF:]
        w_s, w_sT = [sb(f"w_s{i}", [P, P]) for i in range(2)], [sb(f"w_sT{i}", [P, P]) for i in range(2)]
        b_s = sb("b_s", [P, GROUPS])
        us = [sb(f"us{i}", [P, NT, GROUP_DIM]) for i in range(2)]
        stats, moments = sb("stats", [P, NT, 4, 6]), sb("moments", [P, NT, 2])
        ln_var, ln_std, ln_inv = sb("ln_var", [P, NT]), sb("ln_std", [P, NT]), sb("ln_inv", [P, NT])
        mix = g.partial[:].rearrange("p (a b) -> p a b", a=2)
        gate_b = g.squares[0:1, :]
        w_out = [z[:, c // 2, SG_HALF + (c % 2) * D:SG_HALF + (c % 2 + 1) * D] for c in range(8)]
        banks = scope.enter_context(nc.psum_tensor("sg_banks", [P, 8, BANK], FP32))
        ps_s = [banks[:, 2 * i:2 * i + 2, :].rearrange("p a (b c) -> p (a b) c", c=GROUP_DIM) for i in range(2)]
        ps_gate = banks[:, 6:8, :].rearrange("p a b -> p (a b)")
        ps_us, ps_w = banks[:, 4:6, :], banks[:, 6, 0:P]
        sem = g.stage_semaphores(scope, "sg_")
        z_ready, gelu_done, ln_loaded, bs_loaded = sem("z_ready"), sem("gelu_done"), sem("ln_loaded"), sem("bs_loaded")
        ws_loaded, ws_turned, ws_copied = [sem(f"ws_loaded{i}") for i in range(2)], sem("ws_turned"), sem("ws_copied")
        chain_s, var_done, std_done, scaled, shifted = sem("chain"), sem("var_done"), sem("std_done"), sem("scaled"), sem("shifted")
        spatial, gated, us_turned, us_copied = sem("spatial"), sem("gated"), sem("us_turned"), sem("us_copied")
        wo_loaded, wo_used, projected, added = [sem(f"wo_loaded{i}") for i in range(8)], sem("wo_used"), sem("projected"), sem("added")
        ada_loaded, ada_used, ada_chain = [sem(f"ada_loaded{i}") for i in range(2)], sem("ada_used"), sem("ada_chain")
        partial_done, partial_free, partial_stored = sem("partial_done"), sem("partial_free"), g.sem("partial_stored1")
        gate_loaded, gate_summed, gate_done = sem("gate_loaded"), sem("gate_summed"), sem("gate_done")
        g.squared = sem("squared")
        block = scope.enter_context(nc.Block())
        FIRST_ADA, ADA_ROWS = 9, 3
        LN_HOPS = 3

        @block.sync
        def _(sp):
            sp.dma_start(b_s[:], A["sg_b_s"][0, :, :]).then_inc(bs_loaded, 16)
            for i in range(2):
                sp.dma_start(w_s[i][:], A["sg_w_s"][0, i, :, :]).then_inc(ws_loaded[i], 16)
            assert ADA_ROWS == N_IN // 2 - 1
            with sp.Fori(1, N_IN // 2) as r:
                for half in range(2):
                    sp.wait_ge(ada_used, 2 * (r - 1) + half + 1)
                    load_ada(g, sp, FIRST_ADA + r - 1, half, ada_loaded[half])
                for i in range(2):
                    sp.wait_ge(z_ready, 4 * (2 * r + i - 1))
                    load_w_in(g, b, sp, 2 * r + i, i)
            sp.dma_start(gate_b[:], A["ada_b"][1:2, 2 * D:3 * D]).then_inc(gate_loaded, 16)
            sp.wait_ge(partial_free, ADA_ROWS + 1)
            sp.dma_start(g.partial[:], g.mod_dram[8, :, :]).then_inc(gate_loaded, 16)
            sp.wait_ge(z_ready, 4 * N_IN)
            sp.dma_start(ln_g, A["sg_ln_g"][0, :].partition_broadcast(P)).then_inc(ln_loaded, 16)
            sp.dma_start(ln_b, A["sg_ln_b"][0, :].partition_broadcast(P)).then_inc(ln_loaded, 16)
            with sp.Fori(1, GROUPS // 2) as r:
                for i in range(2):
                    sp.wait_ge(ws_turned, 2 * r + i - 1)
                    sp.dma_start(w_s[i][:], A["sg_w_s"][0, ds(2 * r + i, 1), :, :].rearrange("a p q -> p (a q)"))\
                        .then_inc(ws_loaded[i], 16)
            for c in range(K_OUT):
                if c == 0:
                    sp.wait_ge(spatial, GROUPS)
                if c >= 8:
                    sp.wait_ge(wo_used, c - 7)
                sp.dma_start(w_out[c % 8], A["sg_w_out"][0, c * P:(c + 1) * P, :]).then_inc(wo_loaded[c % 8], 16)
            sp.wait_ge(ada_used, 2 * ADA_ROWS + 2)
            g.load_expert(sp, 1, 0, 0)
            g.load_expert(sp, 1, 1, 1)

        @block.gpsimd
        def _(pool):
            pool.sem_clear(g.other_semaphores)
            store_partials(g, pool, FIRST_ADA, ADA_ROWS, partial_done, partial_stored, partial_free)
            pool.wait_ge(ln_loaded, 32)
            with pool.Fori(0, GROUPS) as x:
                pool.wait_ge(scaled, x + 1)
                v = z[:, :, ds(SG_HALF + x * GROUP_DIM, GROUP_DIM)]
                nc.gpsimd.tensor_tensor(v, v, ln_b[:, ds(x * GROUP_DIM, GROUP_DIM)].unsqueeze(1)
                                        .to_broadcast([P, NT, GROUP_DIM]), ALU.add).then_inc(shifted, 1)

        @block.tensor
        def _(pe):
            with pe.Fori(0, N_IN // 2) as r:
                for i in range(2):
                    pe.wait_ge(b.loaded[i], 16 * r + 16)
                    for t in range(NT):
                        pe.wait_ge(gelu_done, 8 * r + 4 * i + t + 1)
                        for k in range(KC):
                            last = nc.tensor.matmul(banks[:, 4 * i + t, :], g.hT[:, k, t * P:(t + 1) * P], b.w_in[i][:, k, :],
                                                    start=(k == 0), stop=(k == KC - 1))
                        last.then_inc(z_ready, 1)

            def turn_w_s(x, i, loads):
                pe.wait_ge(ws_loaded[i], 16 * loads)
                after(pe, ws_copied, x)
                nc.tensor.transpose(ps_w, w_s[i][:], g.ident[:]).then_inc(ws_turned, 1)

            def mix_tokens(x, i):
                pe.wait_ge(shifted, x + 1)
                pe.wait_ge(ws_copied, x + 1)
                pe.wait_ge(gated, x + 1)
                for t in range(NT):
                    last = nc.tensor.matmul(ps_s[i][:, t, :], w_sT[i][:], z[:, t, ds(SG_HALF + x * GROUP_DIM, GROUP_DIM)],
                                            start=True, stop=True)
                last.then_inc(spatial, 1)

            def turn_us(x, i):
                pe.wait_ge(gated, x + 3)
                pe.wait_ge(us_copied, x + 1)
                for j in range(2):
                    for t in range(NT):
                        last = nc.tensor.transpose(ps_us[:, j, t * P:(t + 1) * P], us[i][:, t, j * P:(j + 1) * P], g.ident[:])
                last.then_inc(us_turned, 1)

            pe.sem_inc(us_turned, 2)
            pe.wait_ge(gelu_done, 8 + 4 * N_IN)
            pe.wait_ge(gate_loaded, 32)
            sum_conditioning(nc, g, g.partial, gate_b, ps_gate).then_inc(gate_summed, 1)
            pe.wait_ge(gate_done, 1)
            turn_w_s(0, 0, 1)
            mix_tokens(0, 0)
            turn_w_s(1, 1, 1)
            with pe.Fori(0, GROUPS // 2 - 1) as r:
                for i in range(2):
                    mix_tokens(2 * r + 1 + i, (1 + i) % 2)
                    turn_w_s(2 * r + 2 + i, i, r + 2)
                    turn_us(2 * r + i, i)
            mix_tokens(GROUPS - 1, 1)
            turn_us(GROUPS - 2, 0)
            turn_us(GROUPS - 1, 1)
            pe.wait_ge(us_copied, GROUPS + 1)
            for c in range(K_OUT):
                pe.wait_ge(wo_loaded[c % 8], 16 * (c // 8 + 1))
                for i in range(8):
                    t, n = divmod(i, 2)
                    last = nc.tensor.matmul(banks[:, i, :], usT[:, c, t * P:(t + 1) * P], w_out[c % 8][:, n * BANK:(n + 1) * BANK],
                                            start=(c == 0), stop=(c == K_OUT - 1))
                    if c == K_OUT - 1:
                        last.then_inc(projected, 1)
                if c < K_OUT - 1:
                    last.then_inc(wo_used, 1)

        @block.scalar
        def _(act):
            act.sem_inc(gelu_done, 8)
            act.sem_inc(us_copied, 1)
            with act.Fori(0, N_IN // 2) as r:
                for i in range(2):
                    for t in range(NT):
                        act.wait_ge(z_ready, 8 * r + 4 * i + t + 1)
                        nc.scalar.activation(z[:, t, ds((2 * r + i) * BANK, BANK)], banks[:, 4 * i + t, :], ACT.Gelu)\
                            .then_inc(gelu_done, 1)
            act.wait_ge(gate_summed, 1)
            nc.scalar.activation(g.gate[:], ps_gate, ACT.Copy).then_inc(gate_done, 1)
            act.wait_ge(var_done, 1)
            nc.scalar.activation(ln_std[:], ln_var[:], ACT.Sqrt).then_inc(std_done, 1)

            def copy_w_s(x, i):
                act.wait_ge(ws_turned, x + 1)
                after(act, spatial, x - 1)
                nc.scalar.activation(w_sT[i][:], ps_w, ACT.Copy).then_inc(ws_copied, 1)

            def copy_us(x):
                act.wait_ge(us_turned, x + 3)
                nc.scalar.activation(usT[:, ds(2 * x, 2), :], ps_us, ACT.Copy).then_inc(us_copied, 1)

            copy_w_s(0, 0)
            copy_w_s(1, 1)
            with act.Fori(0, GROUPS // 2 - 1) as r:
                for i in range(2):
                    copy_w_s(2 * r + 2 + i, i)
                    copy_us(2 * r + i)
            copy_us(GROUPS - 2)
            copy_us(GROUPS - 1)
            square_tiles(nc, g, act, added, 2)

        @block.vector
        def _(dve):
            chain = Chain(dve, chain_s)
            dve.sem_inc(gated, 2)
            dve.sem_inc(ada_used, 2)
            with dve.Fori(0, ADA_ROWS) as n:
                dve.wait_ge(partial_free, n + 1)
                for half in range(2):
                    dve.wait_ge(ada_loaded[half], 16 * n + 16)
                    add_ada(nc, g, dve, range(half * ADA_HALF, (half + 1) * ADA_HALF), ada_chain, n, ada_used, partial_done)
            for c in range(4):
                for t in range(NT):
                    dve.wait_ge(gelu_done, 8 + 4 * (4 + c) + t + 1)
                    last = nc.vector.bn_stats(stats[:, t, c, :], z[:, t, SG_HALF + c * BANK:SG_HALF + (c + 1) * BANK])
            chain(last)
            for t in range(NT):
                last = nc.vector.bn_aggr(moments[:, t, :], stats[:, t, :, :].rearrange("p a b -> p (a b)"))
            chain(last)
            nc.vector.tensor_scalar(ln_var[:], moments[:, :, 1], EPS, None, ALU.add).then_inc(var_done, 1)
            dve.wait_ge(std_done, 1)
            chain(nc.vector.reciprocal(ln_inv[:], ln_std[:]))
            dve.wait_ge(ln_loaded, 32)
            dve.wait_ge(bs_loaded, 16)

            def scale_v(x):
                group = Chain(dve, chain_s, LN_HOPS + x)
                for t in range(NT):
                    v = z[:, t, ds(SG_HALF + x * GROUP_DIM, GROUP_DIM)]
                    last = nc.vector.tensor_scalar(v, v, moments[:, t, 0:1], ln_inv[:, t:t + 1], ALU.subtract, ALU.mult)
                group(last)
                v = z[:, :, ds(SG_HALF + x * GROUP_DIM, GROUP_DIM)]
                nc.vector.tensor_tensor(v, v, ln_g[:, ds(x * GROUP_DIM, GROUP_DIM)].unsqueeze(1)
                                        .to_broadcast([P, NT, GROUP_DIM]), ALU.mult).then_inc(scaled, 1)

            def gate_u(x, i):
                dve.wait_ge(spatial, x + 1)
                dve.wait_ge(us_turned, x + 1)
                nc.vector.scalar_tensor_tensor(us[i][:], ps_s[i], b_s[:, ds(x, 1)], z[:, :, ds(x * GROUP_DIM, GROUP_DIM)],
                                               ALU.add, ALU.mult).then_inc(gated, 1)

            assert chain.n == LN_HOPS
            scale_v(0)
            scale_v(1)
            with dve.Fori(0, GROUPS // 2 - 1) as r:
                for i in range(2):
                    gate_u(2 * r + i, i)
                    scale_v(2 * r + 2 + i)
            gate_u(GROUPS - 2, 0)
            gate_u(GROUPS - 1, 1)
            add_gated(nc, g, dve, chain_s, LN_HOPS + GROUPS, projected, added, [banks[:, i, :] for i in range(8)], mix, (gate_done, 1))


def final_norm(nc, g, out):
    with ExitStack() as scope:
        sb = lambda n, s, d=FP32: scope.enter_context(nc.sbuf_tensor(f"fin_{n}", s, d))
        gain, y = sb("gain", [P, D]), sb("y", [P, NT, D])
        mean_sq, std, rstd = sb("mean_sq", [P, NT]), sb("std", [P, NT]), sb("rstd", [P, NT])
        sem = g.stage_semaphores(scope, "fin_")
        gain_loaded, mean_done, std_done = sem("gain_loaded"), sem("mean_done"), sem("std_done")
        inverted, normed, stored = sem("inverted"), sem("normed"), sem("stored")
        block = scope.enter_context(nc.Block())

        @block.gpsimd
        def _(pool):
            pool.sem_clear(g.other_semaphores)

        @block.sync
        def _(sp):
            sp.dma_start(gain[:], g.inputs["final_g"].partition_broadcast(P)).then_inc(gain_loaded, 16)
            for t in range(NT):
                sp.wait_ge(normed, t + 1)
                sp.dma_start(out[0, t * P:(t + 1) * P, :], y[:, t, :]).then_inc(stored, 16)
            sp.wait_ge(stored, 16 * NT)

        @block.scalar
        def _(act):
            act.wait_ge(mean_done, 1)
            nc.scalar.activation(std[:], mean_sq[:], ACT.Sqrt).then_inc(std_done, 1)

        @block.vector
        def _(dve):
            nc.vector.tensor_scalar(mean_sq[:], g.sums[:], 1.0 / D, EPS, ALU.mult, ALU.add).then_inc(mean_done, 1)
            dve.wait_ge(std_done, 1)
            nc.vector.reciprocal(rstd[:], std[:]).then_inc(inverted, 1)
            dve.wait_ge(inverted, 1)
            dve.wait_ge(gain_loaded, 16)
            for t in range(NT):
                nc.vector.scalar_tensor_tensor(y[:, t, :], g.x[:, t, :], rstd[:, t:t + 1], gain[:], ALU.mult, ALU.mult)\
                    .then_inc(normed, 1)


def tokens(nc, name):
    return nc.sbuf_tensor(name, [P, NT, D], FP32)


def build(nc, inputs, out):
    g = Shared()
    g.inputs = inputs
    g.sems = ExitStack()
    with g.sems, ExitStack() as persistent:
        carried = {n: g.sems.enter_context(nc.semaphore(n)) for n in
                   ["q_loaded", "k_loaded", "v_loaded", "wo_loaded", "w_in_loaded0", "w_in_loaded1"] +
                   ["small_loaded", "partial_stored0", "partial_stored1"] +
                   [f"expert_loaded{layer}_{s}" for layer in range(2) for s in range(RING)] +
                   [n.format(layer) for layer in range(2) for n in
                    ("h_stored{}", "over_stored{}", "gathered{}_0", "gathered{}_1", "scattered{}_0", "scattered{}_1",
                     "over_scattered{}")]}
        g.sem = lambda n: carried[n]
        sb = lambda n, s, d=FP32: persistent.enter_context(nc.sbuf_tensor(n, s, d))
        g.x, g.hT, g.gate = sb("x", [P, NT, D]), sb("hT", [P, KC, S]), sb("gate", [P, D])
        g.ring = sb("ring", [P, 2, SLOT])
        g.sums, g.squares = sb("sums", [P, NT]), sb("squares", [P, D])
        g.scale_T, g.shift_T = sb("scale_T", [P, KC]), sb("shift_T", [P, KC])
        g.cond, g.partial = sb("cond", [P, KC]), sb("partial", [P, D])
        g.ident, g.tri, g.ones = sb("ident", [P, P]), sb("tri", [P, P]), sb("ones", [P, P])
        g.group_lower = sb("group_lower", [P, EXPERT_GROUPS, EXPERT_GROUPS])
        g.iota = sb("iota", [P, S])
        g.tok_i = sb("tok_i", [P, NT], I32)
        g.tok, g.tok_shift, g.row_shift = sb("tok", [P, NT]), sb("tok_shift", [P, NT]), sb("row_shift", [P, NT])
        g.prefix = sb("prefix", [P, 2, NT, PAD + E])
        g.mod_dram = nc.dram_tensor("mod_dram", (12, P, D), FP32).ap()
        g.h_dram = nc.dram_tensor("h_dram", (S, D), FP32).ap()
        g.rows_dram = nc.dram_tensor("rows_dram", (S * TOP_K, D), FP32).ap()
        g.over_dram = nc.dram_tensor("over_dram", (P + 1, 2), I32).ap()
        g.expert_loaded = [[g.sem(f"expert_loaded{layer}_{s}") for s in range(RING)] for layer in range(2)]

        def load_expert_into(eng, layer, slot, s, e):
            third = KC * F
            for i, name in enumerate(("moe_w_gate", "moe_w_up")):
                eng.dma_start(slot[:, i * third:(i + 1) * third].rearrange("p (k f) -> p k f", k=KC),
                              inputs[name][layer, ds(e, 1), :, :].rearrange("a (p k) f -> p (a k) f", k=KC))\
                    .then_inc(g.expert_loaded[layer][s], 16)
            eng.dma_start(slot[:, 2 * third:].rearrange("p (j n) -> p j n", j=2),
                          inputs["moe_w_down"][layer, ds(e, 1), :, :].rearrange("a (j p) n -> p (a j) n", p=P))\
                .then_inc(g.expert_loaded[layer][s], 16)

        g.load_expert_into = load_expert_into

        numbers = sorted(nc.free_semaphores)
        half = len(numbers) // 2
        assert numbers[2 * half - 1] - numbers[0] == 2 * half - 1
        sets = [range(numbers[i * half], numbers[i * half] + half) for i in range(2)]
        g.stage = 0

        def stage_semaphores(scope, prefix):
            mine, g.other_semaphores = sets[g.stage % 2], sets[(g.stage + 1) % 2]
            g.stage += 1
            left = iter(mine)
            return lambda n: scope.enter_context(nc.semaphore(prefix + n, num=next(left)))

        g.stage_semaphores = stage_semaphores
        g.load_expert = lambda eng, layer, s, e: load_expert_into(eng, layer, g.ring[:, s, :], s, e)

        with ExitStack() as rope:
            g.cos, g.sin, g.subln, g.neg_lam = (rope.enter_context(nc.sbuf_tensor(n, [P, w], FP32))
                                                for n, w in (("cos", S), ("sin", S), ("subln", 1), ("neg_lam", 1)))
            conditioning(nc, g)
            with ExitStack() as buffers:
                b = attention_buffers(nc, g, buffers)
                with tokens(nc, "n0a_xn") as xn:
                    normalise(nc, g, "n0a", 0, 0, [xn[:, t, :] for t in range(NT)],
                              lambda sp: [load_head(g, b, sp, 0, i) for i in range(3)])
                attention(nc, g, b)
        with ExitStack() as buffers:
            b = experts_buffers(nc, g, 0, buffers)
            normalise(nc, g, "n0b", 0, 1, b.xn, lambda sp: None)
            experts(nc, g, b, 0)
        with ExitStack() as buffers:
            b = gating_buffers(nc, g, buffers)
            with tokens(nc, "n1a_xn") as xn:
                normalise(nc, g, "n1a", 1, 0, [xn[:, t, :] for t in range(NT)],
                          lambda sp: [load_w_in(g, b, sp, i, i) for i in range(2)])
            gating(nc, g, b)
        with ExitStack() as buffers:
            b = experts_buffers(nc, g, 1, buffers)
            normalise(nc, g, "n1b", 1, 1, b.xn, lambda sp: None)
            experts(nc, g, b, 1)
        final_norm(nc, g, out)


_INS = ["x", "c", "positions", "norm1_g", "norm2_g", "ada_w", "ada_b", "da_w_in", "da_lam_q1", "da_lam_k1",
        "da_lam_q2", "da_lam_k2", "da_subln_g", "da_w_out", "sg_w_in", "sg_ln_g", "sg_ln_b", "sg_w_s", "sg_b_s",
        "sg_w_out", "moe_w_router", "moe_router_bias", "moe_w_gate", "moe_w_up", "moe_w_down", "moe_ws_gate",
        "moe_ws_up", "moe_ws_down", "final_g"]


def kernel(**inputs):
    import numpy as np
    import concourse.bacc as bacc
    from concourse import mybir as mb
    from concourse.bass_utils import run_bass_kernel_spmd as run

    nc = bacc.Bacc("TRN2", target_bir_lowering=False, num_devices=1)
    arrays = {name: np.ascontiguousarray(inputs[name]) for name in _INS}
    freq = np.float32(THETA) ** (-np.arange(0, HD, 2, dtype=np.float32) / np.float32(HD))
    arrays["rope_inv_freq"] = np.ascontiguousarray(np.tile(freq.astype(np.float32), 4)[:, None])
    arrays["sg_b_s"] = np.ascontiguousarray(np.swapaxes(arrays["sg_b_s"], 1, 2))
    arrays["ada_w"] = np.ascontiguousarray(np.swapaxes(arrays["ada_w"].reshape(2, D, 6, D), 1, 2).reshape(12, D, D))
    aps = {name: nc.dram_tensor(f"in_{name}", a.shape, mb.dt.from_np(a.dtype), kind="ExternalInput").ap()
           for name, a in arrays.items()}
    out = nc.dram_tensor("out_0", (1, S, D), FP32, kind="ExternalOutput").ap()
    build(nc, aps, out)
    result = run(nc, [{f"in_{name}": a for name, a in arrays.items()}], core_ids=[0])
    return result.results[0]["out_0"]
```
